# Optimizing a Trainium2 kernel written in Bass

```python
import jax, jax.numpy as jnp
from jax import lax
import numpy as np

D_MODEL = 1024
BATCH = 1
SEQ = 256
DEPTH = 2

GRID_W = 64
CTX_LEN = 256
CONV_CH = 256
CONV_WIDTH = 31
NAT_HEADS = 4
NAT_HEAD_DIM = 64
NAT_W = NAT_HEADS * NAT_HEAD_DIM
NAT_KH = 8
NAT_KW = 16
FNET_GROUPS = 4
FNET_GROUP_DIM = 64
FNET_W = FNET_GROUPS * FNET_GROUP_DIM
GQA_Q_HEADS = 8
GQA_KV_HEADS = 2
GQA_HEAD_DIM = 64
GQA_Q_W = GQA_Q_HEADS * GQA_HEAD_DIM
GQA_KV_W = GQA_KV_HEADS * GQA_HEAD_DIM
GQA_WINDOW = 128
GQA_BLOCK = 128
ROPE_BASE = 10000.0
PEER_HEADS = 8
PEER_N_KEYS = 128
PEER_N_EXPERTS = PEER_N_KEYS * PEER_N_KEYS
PEER_TOPK = 16
PEER_D_KEY = 256
PEER_CHUNK = 128
N_BRANCH = 4
LN_EPS = 1e-5
NEG_INF = -1e30
DEEPNORM_ALPHA = (2 * DEPTH) ** 0.25
DEEPNORM_BETA = (8 * DEPTH) ** -0.25
IN_SIZES = (2 * CONV_CH, NAT_W, NAT_W, NAT_W, FNET_W, GQA_Q_W, GQA_KV_W, GQA_KV_W, N_BRANCH * D_MODEL)
IN_TOTAL = sum(IN_SIZES)

kernel_name = "hybrid_parallel_branch_peer_diffusion_block"

def layer_norm(x, g=None, b=None):
    xf = x.astype(jnp.float32)
    mu = jnp.mean(xf, -1, keepdims=True)
    var = jnp.mean(jnp.square(xf - mu), -1, keepdims=True)
    y = (xf - mu) * lax.rsqrt(var + LN_EPS)
    if g is not None:
        y = y * g.astype(jnp.float32) + b.astype(jnp.float32)
    return y.astype(x.dtype)

def modulate(x, shift, scale):
    return layer_norm(x) * (1.0 + scale) + shift

def split_in(p):
    offs = np.cumsum(IN_SIZES)[:-1].tolist()
    return jnp.split(p, offs, axis=-1)

def to_heads(t, h):
    return t.reshape(*t.shape[:-1], h, t.shape[-1] // h)

def conformer_conv(p_conv, conv_w, conv_b, ln_g, ln_b):
    a, g = jnp.split(p_conv, 2, axis=-1)
    h = a * jax.nn.sigmoid(g)
    h = lax.conv_general_dilated(h, conv_w[:, None, :], window_strides=(1,),
                                 padding=[(CONV_WIDTH // 2, CONV_WIDTH // 2)],
                                 dimension_numbers=('NWC', 'WIO', 'NWC'),
                                 feature_group_count=CONV_CH) + conv_b
    return jax.nn.silu(layer_norm(h, ln_g, ln_b))

def fourier_mix(p_f):
    B, T, _ = p_f.shape
    h = p_f.astype(jnp.float32).reshape(B, T, FNET_GROUPS, FNET_GROUP_DIM)
    h = jnp.fft.fftn(h, axes=(1, 3), norm='ortho').real
    return h.reshape(B, T, FNET_W).astype(p_f.dtype)

def axial_rope(x, rows, cols):
    half = x.shape[-1] // 2
    quarter = half // 2
    freqs = ROPE_BASE ** (-jnp.arange(quarter, dtype=jnp.float32) / quarter)

    def rot(xa, pos):
        ang = pos.astype(jnp.float32)[:, None] * freqs
        cos = jnp.cos(ang)[None, :, None, :]
        sin = jnp.sin(ang)[None, :, None, :]
        x1, x2 = xa[..., :quarter], xa[..., quarter:]
        return jnp.concatenate([x1 * cos - x2 * sin, x1 * sin + x2 * cos], -1)

    xf = x.astype(jnp.float32)
    out = jnp.concatenate([rot(xf[..., :half], rows), rot(xf[..., half:], cols)], -1)
    return out.astype(x.dtype)

def context_attention(q, k, v):
    B, L, H, dh = q.shape
    s = jnp.einsum('blhd,bmhd->bhlm', q, k).astype(jnp.float32) * dh ** -0.5
    p = jax.nn.softmax(s, -1).astype(q.dtype)
    return jnp.einsum('bhlm,bmhd->blhd', p, v).reshape(B, L, H * dh)

def neighbourhood_attention(q, k, v, kc, vc, rpb):
    B, S, H, dh = q.shape
    rows = S // GRID_W
    kh = min(NAT_KH, rows)
    scale = dh ** -0.5
    qg = q.reshape(B, rows, GRID_W, H, dh)
    kg = k.reshape(B, rows, GRID_W, H, dh)
    vg = v.reshape(B, rows, GRID_W, H, dh)
    col = jnp.arange(GRID_W)
    cstart = jnp.clip(col - NAT_KW // 2, 0, GRID_W - NAT_KW)
    cidx = cstart[:, None] + jnp.arange(NAT_KW)[None, :]
    dc = cidx - col[:, None] + (NAT_KW - 1)

    def one_row(r):
        rstart = jnp.clip(r - kh // 2, 0, rows - kh)
        q_r = lax.dynamic_index_in_dim(qg, r, axis=1, keepdims=False)
        k_band = lax.dynamic_slice_in_dim(kg, rstart, kh, axis=1)
        v_band = lax.dynamic_slice_in_dim(vg, rstart, kh, axis=1)
        k_nb = k_band[:, :, cidx]
        v_nb = v_band[:, :, cidx]
        dr = rstart + jnp.arange(kh) - r + (NAT_KH - 1)
        bias = rpb[:, dr][:, :, dc].transpose(0, 2, 1, 3)
        s_nb = jnp.einsum('bchd,bwckhd->bhcwk', q_r, k_nb).astype(jnp.float32) * scale
        s_nb = (s_nb + bias[None].astype(jnp.float32)).reshape(B, H, GRID_W, kh * NAT_KW)
        s_ctx = jnp.einsum('bchd,blhd->bhcl', q_r, kc).astype(jnp.float32) * scale
        probs = jax.nn.softmax(jnp.concatenate([s_nb, s_ctx], -1), -1).astype(q.dtype)
        p_nb = probs[..., :kh * NAT_KW].reshape(B, H, GRID_W, kh, NAT_KW)
        p_ctx = probs[..., kh * NAT_KW:]
        return (jnp.einsum('bhcwk,bwckhd->bchd', p_nb, v_nb)
                + jnp.einsum('bhcl,blhd->bchd', p_ctx, vc))

    out = lax.map(one_row, jnp.arange(rows))
    return out.transpose(1, 0, 2, 3, 4).reshape(B, S, H * dh)

def window_gqa_latent(q, k, v, kc, vc, sink):
    B, S, _, dh = q.shape
    G = GQA_KV_HEADS
    R = GQA_Q_HEADS // G
    L = kc.shape[1]
    nb = S // GQA_BLOCK
    scale = dh ** -0.5
    qb = q.reshape(B, nb, GQA_BLOCK, G, R, dh)
    pad = ((0, 0), (GQA_BLOCK, GQA_BLOCK), (0, 0), (0, 0))
    kp = jnp.pad(k, pad).reshape(B, nb + 2, GQA_BLOCK, G, dh)
    vp = jnp.pad(v, pad).reshape(B, nb + 2, GQA_BLOCK, G, dh)
    kband = jnp.concatenate([kp[:, :-2], kp[:, 1:-1], kp[:, 2:]], axis=2)
    vband = jnp.concatenate([vp[:, :-2], vp[:, 1:-1], vp[:, 2:]], axis=2)
    qpos = jnp.arange(S).reshape(nb, GQA_BLOCK)
    kpos = jnp.arange(nb)[:, None] * GQA_BLOCK - GQA_BLOCK + jnp.arange(3 * GQA_BLOCK)[None, :]
    kp3 = kpos[:, None, :]
    valid = (jnp.abs(kp3 - qpos[:, :, None]) <= GQA_WINDOW) & (kp3 >= 0) & (kp3 < S)
    s_band = jnp.einsum('bnqgrd,bnkgd->bgrnqk', qb, kband).astype(jnp.float32) * scale
    s_band = jnp.where(valid, s_band, NEG_INF)
    s_ctx = jnp.einsum('bnqgrd,blgd->bgrnql', qb, kc).astype(jnp.float32) * scale
    s_sink = jnp.broadcast_to(sink.astype(jnp.float32).reshape(1, G, R, 1, 1, 1),
                              (B, G, R, nb, GQA_BLOCK, 1))
    probs = jax.nn.softmax(jnp.concatenate([s_band, s_ctx, s_sink], -1), -1).astype(q.dtype)
    nk = 3 * GQA_BLOCK
    out = (jnp.einsum('bgrnqk,bnkgd->bnqgrd', probs[..., :nk], vband)
           + jnp.einsum('bgrnql,blgd->bnqgrd', probs[..., nk:nk + L], vc))
    return out.reshape(B, S, GQA_Q_HEADS * dh)

def gqa_context(q, k, v, sink):
    B, L, _, dh = q.shape
    G = GQA_KV_HEADS
    R = GQA_Q_HEADS // G
    qg = q.reshape(B, L, G, R, dh)
    s = jnp.einsum('blgrd,bmgd->bgrlm', qg, k).astype(jnp.float32) * dh ** -0.5
    s_sink = jnp.broadcast_to(sink.astype(jnp.float32).reshape(1, G, R, 1, 1), (B, G, R, L, 1))
    probs = jax.nn.softmax(jnp.concatenate([s, s_sink], -1), -1)[..., :L].astype(q.dtype)
    return jnp.einsum('bgrlm,bmgd->blgrd', probs, v).reshape(B, L, GQA_Q_HEADS * dh)

def merge_branches(y_a, y_b, y_c, y_d, gate_logits, w_a, w_b, w_c, w_d, w_o):
    g = jax.nn.sigmoid(gate_logits).reshape(*gate_logits.shape[:-1], N_BRANCH, D_MODEL)
    m = (g[..., 0, :] * (y_a @ w_a) + g[..., 1, :] * (y_b @ w_b)
         + g[..., 2, :] * (y_c @ w_c) + g[..., 3, :] * (y_d @ w_d))
    return m @ w_o

def peer_ffn(u, wq, k1, k2, eu, ev):
    B, T, D = u.shape
    xs = u.reshape(-1, PEER_CHUNK, D)
    half = PEER_D_KEY // 2

    def chunk(xc):
        q = (xc @ wq).reshape(PEER_CHUNK, PEER_HEADS, 2, half)
        s1 = jnp.einsum('thd,hnd->thn', q[:, :, 0], k1).astype(jnp.float32)
        s2 = jnp.einsum('thd,hnd->thn', q[:, :, 1], k2).astype(jnp.float32)
        v1, i1 = lax.top_k(s1, PEER_TOPK)
        v2, i2 = lax.top_k(s2, PEER_TOPK)
        cand = (v1[..., :, None] + v2[..., None, :]).reshape(PEER_CHUNK, PEER_HEADS, -1)
        cidx = (i1[..., :, None] * PEER_N_KEYS + i2[..., None, :]).reshape(PEER_CHUNK, PEER_HEADS, -1)
        top_s, pos = lax.top_k(cand, PEER_TOPK)
        eidx = jnp.take_along_axis(cidx, pos, -1)
        g = jax.nn.softmax(top_s, -1).astype(xc.dtype)
        h = jax.nn.gelu(jnp.einsum('thkd,td->thk', eu[eidx], xc), approximate=False)
        return jnp.einsum('thk,thkd->td', g * h, ev[eidx])

    return lax.map(chunk, xs).reshape(B, T, D)

def setup_inputs(seed: int = 0) -> dict:
    key = jax.random.key(seed)
    ks = jax.random.split(key, 28)
    f32 = jnp.float32
    D = D_MODEL
    L = DEPTH

    def nrm(k, shape, s):
        return jax.random.normal(k, shape, f32) * s

    return {
        "x": nrm(ks[0], (BATCH, SEQ, D), 1.0),
        "c": nrm(ks[1], (BATCH, D), 1.0),
        "ctx": nrm(ks[2], (BATCH, CTX_LEN, D), 1.0),
        "c_ctx": nrm(ks[3], (D,), 1.0),
        "w_ada": nrm(ks[4], (L, D, 6 * D), D ** -0.5),
        "b_ada": nrm(ks[5], (L, 6 * D), 0.01),
        "w_in": nrm(ks[6], (L, D, IN_TOTAL), D ** -0.5),
        "b_in": nrm(ks[7], (L, IN_TOTAL), 0.01),
        "conv_w": nrm(ks[8], (L, CONV_WIDTH, CONV_CH), CONV_WIDTH ** -0.5),
        "conv_b": nrm(ks[9], (L, CONV_CH), 0.01),
        "conv_ln_g": 1.0 + nrm(ks[10], (L, CONV_CH), 0.1),
        "conv_ln_b": nrm(ks[11], (L, CONV_CH), 0.01),
        "nat_rpb": nrm(ks[12], (L, NAT_HEADS, 2 * NAT_KH - 1, 2 * NAT_KW - 1), 0.1),
        "gqa_sink": nrm(ks[13], (L, GQA_Q_HEADS), 1.0),
        "w_branch_a": nrm(ks[14], (L, CONV_CH, D), CONV_CH ** -0.5),
        "w_branch_b": nrm(ks[15], (L, NAT_W, D), NAT_W ** -0.5),
        "w_branch_c": nrm(ks[16], (L, FNET_W, D), FNET_W ** -0.5),
        "w_branch_d": nrm(ks[17], (L, GQA_Q_W, D), GQA_Q_W ** -0.5),
        "w_out": nrm(ks[18], (L, D, D), D ** -0.5 * DEEPNORM_BETA),
        "ln1_g": 1.0 + nrm(ks[19], (L, D), 0.1),
        "ln1_b": nrm(ks[20], (L, D), 0.01),
        "peer_wq": nrm(ks[21], (L, D, PEER_HEADS * PEER_D_KEY), D ** -0.5),
        "peer_k1": nrm(ks[22], (L, PEER_HEADS, PEER_N_KEYS, PEER_D_KEY // 2), (PEER_D_KEY // 2) ** -0.5),
        "peer_k2": nrm(ks[23], (L, PEER_HEADS, PEER_N_KEYS, PEER_D_KEY // 2), (PEER_D_KEY // 2) ** -0.5),
        "peer_u": nrm(ks[24], (L, PEER_N_EXPERTS, D), D ** -0.5),
        "peer_v": nrm(ks[25], (L, PEER_N_EXPERTS, D), DEEPNORM_BETA),
        "ln2_g": 1.0 + nrm(ks[26], (L, D), 0.1),
        "ln2_b": nrm(ks[27], (L, D), 0.01),
    }

def reference(x, c, ctx, c_ctx, w_ada, b_ada, w_in, b_in, conv_w, conv_b, conv_ln_g, conv_ln_b,
              nat_rpb, gqa_sink, w_branch_a, w_branch_b, w_branch_c, w_branch_d, w_out,
              ln1_g, ln1_b, peer_wq, peer_k1, peer_k2, peer_u, peer_v, ln2_g, ln2_b):
    S = x.shape[1]
    t = jnp.arange(S)
    pos_row = t // GRID_W
    pos_col = t % GRID_W
    xc = ctx
    for i in range(DEPTH):
        mod_l = (jax.nn.silu(c) @ w_ada[i] + b_ada[i])[:, None, :]
        mod_c = jax.nn.silu(c_ctx) @ w_ada[i] + b_ada[i]
        sh1_l, sc1_l, g1_l, sh2_l, sc2_l, g2_l = jnp.split(mod_l, 6, axis=-1)
        sh1_c, sc1_c, g1_c, sh2_c, sc2_c, g2_c = jnp.split(mod_c, 6, axis=-1)

        pc = modulate(xc, sh1_c, sc1_c) @ w_in[i] + b_in[i]
        c_conv, c_nq, c_nk, c_nv, c_f, c_gq, c_gk, c_gv, c_gate = split_in(pc)
        nk_c = to_heads(c_nk, NAT_HEADS)
        nv_c = to_heads(c_nv, NAT_HEADS)
        gk_c = to_heads(c_gk, GQA_KV_HEADS)
        gv_c = to_heads(c_gv, GQA_KV_HEADS)

        pl = modulate(x, sh1_l, sc1_l) @ w_in[i] + b_in[i]
        l_conv, l_nq, l_nk, l_nv, l_f, l_gq, l_gk, l_gv, l_gate = split_in(pl)
        y_a = conformer_conv(l_conv, conv_w[i], conv_b[i], conv_ln_g[i], conv_ln_b[i])
        y_b = neighbourhood_attention(to_heads(l_nq, NAT_HEADS), to_heads(l_nk, NAT_HEADS),
                                      to_heads(l_nv, NAT_HEADS), nk_c, nv_c, nat_rpb[i])
        y_c = fourier_mix(l_f)
        y_d = window_gqa_latent(axial_rope(to_heads(l_gq, GQA_Q_HEADS), pos_row, pos_col),
                                axial_rope(to_heads(l_gk, GQA_KV_HEADS), pos_row, pos_col),
                                to_heads(l_gv, GQA_KV_HEADS), gk_c, gv_c, gqa_sink[i])
        mix = merge_branches(y_a, y_b, y_c, y_d, l_gate, w_branch_a[i], w_branch_b[i],
                             w_branch_c[i], w_branch_d[i], w_out[i])
        x = layer_norm(DEEPNORM_ALPHA * x + g1_l * mix, ln1_g[i], ln1_b[i])
        ffn = peer_ffn(modulate(x, sh2_l, sc2_l), peer_wq[i], peer_k1[i], peer_k2[i], peer_u[i], peer_v[i])
        x = layer_norm(DEEPNORM_ALPHA * x + g2_l * ffn, ln2_g[i], ln2_b[i])

        if i < DEPTH - 1:
            yc_a = conformer_conv(c_conv, conv_w[i], conv_b[i], conv_ln_g[i], conv_ln_b[i])
            yc_b = context_attention(to_heads(c_nq, NAT_HEADS), nk_c, nv_c)
            yc_c = fourier_mix(c_f)
            yc_d = gqa_context(to_heads(c_gq, GQA_Q_HEADS), gk_c, gv_c, gqa_sink[i])
            mix_c = merge_branches(yc_a, yc_b, yc_c, yc_d, c_gate, w_branch_a[i], w_branch_b[i],
                                   w_branch_c[i], w_branch_d[i], w_out[i])
            xc = layer_norm(DEEPNORM_ALPHA * xc + g1_c * mix_c, ln1_g[i], ln1_b[i])
            ffn_c = peer_ffn(modulate(xc, sh2_c, sc2_c), peer_wq[i], peer_k1[i], peer_k2[i],
                             peer_u[i], peer_v[i])
            xc = layer_norm(DEEPNORM_ALPHA * xc + g2_c * ffn_c, ln2_g[i], ln2_b[i])
    return x


_drawn_inputs = setup_inputs


def setup_inputs(seed=0):
    import zlib

    import numpy as np

    out = dict(_drawn_inputs(seed))
    spreads = {}
    factors = {'b_in': 4.754,
     'conv_b': 16.24,
     'conv_ln_b': 22.208,
     'nat_rpb': 5.342,
     'gqa_sink': 8.0,
     'ln2_b': 2.857}
    for name, (base, spread) in spreads.items():
        noise = np.random.default_rng([zlib.crc32(name.encode()), seed]).standard_normal(out[name].shape)
        drawn = base * np.exp(spread * noise) if base else spread * noise
        out[name] = __import__('jax').numpy.asarray(drawn.astype(out[name].dtype))
    for name, factor in factors.items():
        out[name] = (out[name] * factor).astype(out[name].dtype)
    return out
```

```python
import concourse.bass as bass
from concourse import mybir
from contextlib import ExitStack

F32 = mybir.dt.float32
BF16 = mybir.dt.bfloat16
U32 = mybir.dt.uint32
ALU = mybir.AluOpType
ACT = mybir.ActivationFunctionType
AX = mybir.AxisListType.X

D = 1024
P = 128
TOK = 256
TT = TOK // P
KD = D // P
DEPTH = 2
GRID_W = 64
ROWS = TOK // GRID_W
TAPS = 31
DH = 64
NAT_H, GQA_H = 4, 8
RPB_W = 31
BANDS = 2 * ROWS - 1
PADW = 96
NAT_DR = 15
NB = 4
HEADS, TOPK, NKEY = 8, 16, 128
SEG = 2 * HEADS
LN_EPS = 1e-5
ALPHA = (2 * DEPTH) ** 0.25
SCALE = DH ** -0.5
LOWEST = -3.0e38
C_NQ, C_NV, C_GQ, C_GK, C_GV, C_GATE = 4, 8, 12, 16, 17, 18
R_ADA, R_CB, R_CG, R_CLB, R_GQ, R_END = 50, 98, 100, 102, 104, 108
GRP = 4
RING = 8
WBLK = 42

PASSES = [("ctx0", 0, 1, False), ("lat0", 0, 0, False), ("kv1", 1, 1, True), ("lat1", 1, 0, False)]


class Weights:

    def __init__(self):
        self.n = 0
        self.landed = [0, 0]

    def next(self, dmas):
        slot = self.n % 2
        self.n += 1
        self.landed[slot] += 16 * dmas
        return slot, self.landed[slot]

    def skip(self, tiles, dmas):
        for _ in range(tiles):
            self.next(dmas)


class Chain:

    def __init__(self, eng, sem):
        self.eng, self.sem, self.n, self.off = eng, sem, 0, None

    def add(self, ins):
        self.n += 1
        ins.then_inc(self.sem, 1)
        return ins

    def wait(self):
        self.eng.wait_ge(self.sem, self.n if self.off is None else self.off + self.n)

    def link(self, ins):
        self.add(ins)
        self.wait()

    def loop(self, i, per):
        self.off, self.per, self.at = i * per, per, self.n

    def end(self, turns):
        assert self.n - self.at == self.per, (self.n, self.at, self.per)
        self.n += self.per * (turns - 1)
        self.off = None


def units_of(stream, kv):
    if kv:
        return [("T", 1, 2, ("nk", 0)), ("T", 1, 3, ("nk", 1)), ("N", 2, 0, 0), ("N", 2, 0, 1),
                ("T", 4, 0, ("gk", 0)), ("V", 4, 1, 0), ("V", 4, 1, 1)]
    u = [("T", 0, j, ("cv", j)) for j in range(4)]
    u += [("T", 1, j, (("nq", "nk")[j // 2], j % 2)) for j in range(4)]
    u += [("N", 2, 0, 0), ("N", 2, 0, 1)]
    u += [("Q", 3, j, ("gq", j)) for j in range(4)]
    u += [("T", 4, 0, ("gk", 0)), ("V", 4, 1, 0), ("V", 4, 1, 1)]
    return u


def attention_jobs():
    return [(br, h, qt) for br, heads in ((0, NAT_H), (1, GQA_H)) for h in range(heads) for qt in range(TT)]


def build(nc, x, c, ctx, c_ctx, w_ada, b_ada, w_in, b_in, conv_w, conv_b, conv_ln_g, conv_ln_b, nat_rpb,
          gqa_sink, w_branch_a, w_branch_b, w_branch_c, w_branch_d, w_out, ln1_g, ln1_b, peer_wq, peer_k1,
          peer_k2, peer_u0, peer_u1, peer_v0, peer_v1, ln2_g, ln2_b, ident_c, dft_c, dftg_c, rope_c, rot_c, mask_c, iota_c, out):
    es = ExitStack()
    with es:
        def sb(name, shape, dt=F32):
            return es.enter_context(nc.sbuf_tensor(name, shape, dt))

        def sem(name):
            return es.enter_context(nc.semaphore(name))

        arena = sb("arena", [P, 2 * RING * D])
        um = sb("um", [P, 2 * KD * TOK])

        def part(at, shape, dt=F32, of=arena):
            n = 1
            for d_ in shape:
                n *= d_
            v = of[:, at:at + n]
            if dt != F32:
                v = v.bitcast(dt)
            if len(shape) == 2:
                v = v.rearrange("p (a b) -> p a b", a=shape[0])
            elif len(shape) == 3:
                v = v.rearrange("p (a b c) -> p a b c", a=shape[0], b=shape[1])
            return v, at + n

        X = sb("X", [P, 2, TT, D])
        scratch = sb("scratch", [P, TT, D])
        oT = sb("oT", [P, KD, TOK])
        W = sb("W", [P, 2, WBLK * P])
        ident = sb("ident", [P, P])
        dft = sb("dft", [P, TT, 2, TOK])
        dftg = sb("dftg", [P, 2, P])
        rope = sb("rope", [P, 2, TOK])
        rot = sb("rot", [P, P])
        masks = sb("masks", [P, TT, 2, TOK])
        iota = sb("iota", [P, TOPK])
        ones = sb("ones", [P, P])
        onesb = sb("onesb", [P, P], BF16)
        eps = sb("eps", [P, 1])
        cols = sb("cols", [P, 5, P])
        silu_c = sb("silu_c", [P, KD, 2])
        mod = sb("mod", [P, 48, 2])
        lnrow = sb("lnrow", [P, 2, D])
        brow = sb("brow", [P, 5 * P])
        sink = sb("sink", [P, GQA_H])
        bias = sb("bias", [P, TT, NAT_H, TOK])
        hpad = sb("hpad", [P, 2, TOK + TAPS - 1])
        nkb_c = sb("nkb_c", [P, 2, TOK])
        gkc = sb("gkc", [P, TOK])
        nvf_c = sb("nvf_c", [P, TT, 4 * P])
        gvb_c = sb("gvb_c", [P, TT, P])
        st8 = sb("st8", [P, 2, 8])
        bst = sb("bst", [P, 2, 6])
        mv = sb("mv", [P, 2])
        sd = sb("sd", [P, 2])
        gT = sb("gT", [P, TOK])
        eT = sb("eT", [P, TOK], U32)
        zcol = sb("zcol", [P, 2, GRP, 32])
        hcol = sb("hcol", [P, 2, GRP])
        ge = sb("ge", [P, 2, GRP])
        eidx = sb("eidx", [P, 2, 2, GRP], U32)
        cv, at = part(0, [4, TOK])
        hacc, at = part(at, [2, TOK])
        hsq, at = part(at, [2, TOK])
        hstd, at = part(at, [TOK])
        nq, at = part(at, [2, TOK])
        gqk, at = part(at, [5, TOK])
        yb, at = part(at, [10, TOK])
        fs, at = part(at, [2, 2, TOK])
        Sm, at = part(at, [2, 2 * TOK])
        Pn, at = part(at, [2, 2 * TOK])
        PT, at = part(at, [2, 2 * TOK])
        sg, at = part(at, [2, TOK])
        prod, at = part(at, [2, TOK])
        nkb_l, at = part(at, [2, TOK])
        nvf_l, at = part(at, [TT, 4 * P])
        gvb_l, at = part(at, [TT, P])
        nkb, nvf, gvb = [nkb_l, nkb_c], [nvf_l, nvf_c], [gvb_l, gvb_c]
        assert at <= 8 * 2048
        qT, _ = part(0, [SEG, TOK])
        big = [part(q * 2048, [2048])[0] for q in (2, 3, 6, 7)]
        kT, at = part(4 * 2048, [SEG, NKEY])
        v16, at = part(at, [SEG, TOPK])
        i16, at = part(at, [SEG, TOPK], U32)
        i16f, at = part(at, [SEG, TOPK])
        ts, at = part(at, [HEADS, TOPK])
        pos, at = part(at, [HEADS, TOPK], U32)
        ab, at = part(at, [2, HEADS * TOPK], U32)
        abf, at = part(at, [2, HEADS * TOPK])
        isel, at = part(at, [2, HEADS * TOPK])
        hsum, at = part(at, [2, HEADS])
        assert at <= 6 * 2048
        Ur, at = part(0, [RING, D])
        Vr, at = part(at, [RING, D])
        uT, at = part(0, [KD, TOK], of=um)
        mT, _ = part(at, [KD, TOK], of=um)
        xs = um[:, at:at + 3 * D // 2].bitcast(BF16).rearrange("p (a b) -> p a b", a=3)
        xr = um[0:3, :].bitcast(BF16).rearrange("p (a b) -> p a b", a=2)
        ystage = oT[0:GRP, :, :].rearrange("p k t -> p (k t)").rearrange("p (h d) -> p h d", h=2)
        yrows, _ = part(0, [TT, D], of=um)
        rows, _ = part(0, [5, P], of=scratch[:, :, :].rearrange("p t d -> p (t d)"))
        ones3 = onesb[0:3, :]
        PS = es.enter_context(nc.psum_tensor("PS", [P, 8 * 512], F32))
        junk = scratch[:, 0, :]
        xrows = nc.dram_tensor("xrows", [3, TOK, 3, D], BF16, kind="Internal").ap()
        ysum = nc.dram_tensor("ysum", [3, TOK, D], F32, kind="Internal").ap()
        spread_b = nc.dram_tensor("spread_b", [DEPTH, NAT_H, BANDS, GRID_W, PADW], F32, kind="Internal")
        ZROWS = DEPTH * NAT_H * BANDS * 2
        ZCOLS = GRID_W * PADW // 2

        def bank(i, a=0, b=512):
            return PS[:, i * 512 + a:i * 512 + b]

        consts = sem("consts_landed")
        set_up = sem("memsets_done")
        rows_t = sem("rows_transposed")
        cols_s = sem("columns_ready")
        silu_s = sem("silu_ready")
        padz = sem("rpb_zeroed")
        padr = sem("rpb_padded")
        w_land = [sem("weights_landed0"), sem("weights_landed1")]
        w_used = sem("weights_used")
        mod_p = sem("mod_product")
        mod_s = sem("mod_ready")
        lrow_s = sem("layer_rows_landed")
        ln_land = sem("norm_rows_landed")
        bias_s = sem("bias_landed")
        biasm_s = sem("bias_masked")
        dch_s = sem("vector_chain")
        ach_s = sem("scalar_chain")
        FP = [0, 1, 3]
        per_pass = dict(
            stat=2 * TT, std=2 * TT, xn=2 * TT, xnT=2 * TT, u_ready=2 * TT,
            unit=23, unit_act=19, unit_dve=4,
            ropemm=1, roped=1, S=24, sm=24, exp=24, pn=24, ptp=24, pts=24, O=24, y=24,
            conv_done=1, cmean=1, csq=1, cvar=1, cstd=1, cnorm=1, ya=1,
            gate=32, sig=32, merged=34, macc=8, wo=24, wo_s=24,
            resT=TT + 1, rstat=2 * TT, rstd=2 * TT, x_new=2 * TT,
            urow=TT, xsplit=TT, xs_dram=16 * TT, keysT=1, keys_s=4, sc_ps=8, sc_s=8,
            tsub=TT, texp=TT, sel=TT, selT=TT, sel_s=2 * TT, g2=1)
        keys_only = dict(stat=TT, std=TT, xn=TT, xnT=TT, u_ready=TT, unit=7, unit_act=3, unit_dve=4)
        stage = {n: sem(n) for n in per_pass}

        class Pass:

            def __init__(self, p):
                self.base = {}
                for n, c_ in per_pass.items():
                    made = [keys_only.get(n, 0) if PASSES[q][3] else
                            0 if n in ("ropemm", "roped") and PASSES[q][2] else c_ for q in range(p)]
                    self.base[n] = sum(made)

            def __getitem__(self, n):
                return stage[n]

            def at(self, n, v):
                return v + self.base[n]

        R = [Pass(p) for p in range(len(PASSES))]
        u_land = [sem(f"u_rows_landed{k}") for k in range(RING)]
        v_land = [sem(f"v_rows_landed{k}") for k in range(RING)]
        u_free = sem("u_slots_freed")
        v_free = sem("v_slots_freed")
        u_staged = sem("u_row_numbers_staged")
        v_staged = sem("v_row_numbers_staged")
        asked = sem("rows_asked")
        xr_land = [sem("x_rows_landed0"), sem("x_rows_landed1")]
        xr_free = sem("x_rows_freed")
        xb_s = sem("x_broadcast")
        gelu_s = sem("gelu_done")
        w_s = sem("expert_weights_ready")
        y_out = [sem("sums_written0"), sem("sums_written1")]
        y_in = sem("sums_landed")
        yc_s = sem("expert_sums_copied")
        out_s = sem("out_written")
        block = es.enter_context(nc.Block())

        NG = TOK // GRP // 2

        def full_index(p):
            return FP.index(p)

        @block.sync
        def _(sp):
            wt = Weights()

            def wtile(dsts, turn=None, first=None):
                n = wt.n
                slot, _ = wt.next(len(dsts))
                sp.wait_ge(w_used, n + 1 if turn is None else turn * 2 + (n + 1))
                for dst, src in dsts:
                    sp.dma_start(dst(slot), src).then_inc(w_land[slot], 16)

            def slot_view(blocks, width, at=0):
                return lambda s: W[:, s, at * P:at * P + blocks * width].rearrange("p (k n) -> p k n", k=blocks)

            xv = x[0].rearrange("(t p) d -> p t d", p=P)
            cxv = ctx[0].rearrange("(t p) d -> p t d", p=P)
            for dst, src in [(X[:, 0], xv), (X[:, 1], cxv), (ident[:, :], ident_c), (dft[:, :, :, :], dft_c),
                             (dftg[:, :, :], dftg_c), (rope[:, :, :], rope_c), (rot[:, :], rot_c),
                             (masks[:, :, :, :], mask_c),
                             (iota[:, :], iota_c),
                             (rows[0:8, 4, :], c.rearrange("a (k p) -> (a k) p", p=P)),
                             (rows[8:16, 4, :], c_ctx.rearrange("(k p) -> k p", p=P))]:
                sp.dma_start(dst, src).then_inc(consts, 16)
            for l in range(DEPTH):
                a = 2 * l
                for dst, src in [(rows[0:50, a, :], b_in[l].rearrange("(k p) -> k p", p=P)),
                                 (rows[R_ADA:R_CB, a, :], b_ada[l].rearrange("(k p) -> k p", p=P)),
                                 (rows[R_CB:R_CG, a, :], conv_b[l].rearrange("(k p) -> k p", p=P)),
                                 (rows[R_CG:R_CLB, a, :], conv_ln_g[l].rearrange("(k p) -> k p", p=P)),
                                 (rows[R_CLB:R_GQ, a, :], conv_ln_b[l].rearrange("(k p) -> k p", p=P)),
                                 (rows[R_GQ:R_END, a, :].rearrange("p (g d) -> p g d", g=2),
                                  b_in[l, C_GQ * P:C_GK * P].rearrange("(g h d) -> h g d", g=2, h=4)),
                                 (rows[0:2 * TAPS, a + 1, :], conv_w[l].rearrange("t (k p) -> (t k) p", p=P))]:
                    sp.dma_start(dst, src).then_inc(consts, 16)
            sp.wait_ge(set_up, 1)
            sp.dma_start(spread_b.ap().rearrange("l h b (e c) w -> (l h b e) (c w)", e=2),
                         um[0:ZROWS, 0:ZCOLS]).then_inc(padz, 16)
            sp.wait_ge(padz, 16)
            lo = NAT_DR // 2 - (ROWS - 1)
            for l in range(DEPTH):
                for h in range(NAT_H):
                    src = nat_rpb[l, h, lo:lo + BANDS, :].unsqueeze(1).to_broadcast([BANDS, GRID_W, RPB_W])
                    dst = bass.AP(spread_b, (l * NAT_H + h) * BANDS * GRID_W * PADW,
                                  [[GRID_W * PADW, BANDS], [PADW + 1, GRID_W], [1, RPB_W]])
                    sp.dma_start(dst, src).then_inc(padr, 16)
            sp.wait_ge(padr, 16 * DEPTH * NAT_H)

            def layer_rows(l):
                if l:
                    sp.wait_ge(R[1]["y"], R[1].at("y", 24))
                sp.dma_start(brow[:, 0:4 * P], b_in[l, C_NV * P:C_GQ * P].partition_broadcast(P)).then_inc(lrow_s, 16)
                sp.dma_start(brow[:, 4 * P:5 * P],
                             b_in[l, C_GV * P:C_GATE * P].partition_broadcast(P)).then_inc(lrow_s, 16)
                sp.dma_start(sink[:, :], gqa_sink[l].partition_broadcast(P)).then_inc(lrow_s, 16)
                for r in range(ROWS):
                    for h in range(NAT_H):
                        src = bass.AP(spread_b, ((l * NAT_H + h) * BANDS + ROWS - 1 - r) * GRID_W * PADW + RPB_W // 2,
                                      [[PADW, GRID_W], [GRID_W * PADW, ROWS], [1, GRID_W]])
                        dst = bias[(r % 2) * GRID_W:(r % 2 + 1) * GRID_W, r // 2, h, :]
                        sp.dma_start(dst.rearrange("p (w c) -> p w c", w=ROWS), src).then_inc(bias_s, 16)

            def ada(l):
                v = w_ada[l].rearrange("(k p) n -> p k n", p=P)
                with sp.Fori(0, 6) as i:
                    for h in range(2):
                        wtile([(slot_view(KD, 512), v[:, :, bass.ds(i * 1024 + h * 512, 512)])], i)
                wt.skip(10, 1)

            lns = [0]

            def ln_rows(g, b, q, tiles):
                if lns[0]:
                    sp.wait_ge(R[q]["x_new"], R[q].at("x_new", tiles))
                lns[0] += 1
                sp.dma_start(lnrow[:, 0, :], g.partition_broadcast(P)).then_inc(ln_land, 16)
                sp.dma_start(lnrow[:, 1, :], b.partition_broadcast(P)).then_inc(ln_land, 16)

            for p, (name, l, s, kv) in enumerate(PASSES):
                if p in (0, 2):
                    layer_rows(l)
                    ada(l)
                wi = w_in[l].rearrange("(k p) n -> p k n", p=P)
                if kv:
                    for t in (1, 2):
                        wtile([(slot_view(KD, 512), wi[:, :, t * 512:(t + 1) * 512])])
                else:
                    for t in range(3):
                        wtile([(slot_view(KD, 512), wi[:, :, t * 512:(t + 1) * 512])])
                    wtile([(lambda s_, g=g, j=j: W[:, s_, 0:KD * 512].rearrange(
                        "p (k h g d) -> p k h g d", k=KD, h=4, g=2)[:, :, j, g, :],
                        wi[:, :, C_GQ * P + (g * 4 + j) * DH:C_GQ * P + (g * 4 + j + 1) * DH])
                        for g in range(2) for j in range(4)])
                wtile([(slot_view(KD, 256), wi[:, :, 2048:2304])])
                if kv:
                    continue
                gv = wi[:, :, C_GATE * P:].rearrange("p k (b n) -> p k b n", b=NB)
                br = [w[l].rearrange("(k p) n -> p k n", p=P) for w in (w_branch_a, w_branch_b, w_branch_c, w_branch_d)]
                with sp.Fori(0, 4) as i:
                    for h in range(2):
                        j = bass.ds(i * (2 * P) + h * P, P)
                        dsts, at = [], 32
                        for b in range(NB):
                            dsts.append((lambda s, b=b: W[:, s, 0:32 * P].rearrange(
                                "p (k b n) -> p k b n", k=KD, b=NB)[:, :, b, :], gv[:, :, b, j]))
                        for w, kt in zip(br, (2, 2, 2, 4)):
                            dsts.append((slot_view(kt, P, at), w[:, :, j]))
                            at += kt
                        wtile(dsts, i)
                wt.skip(6, 8)
                wo = w_out[l].rearrange("(k p) n -> p k n", p=P)
                for t in range(2):
                    wtile([(slot_view(KD, 512), wo[:, :, t * 512:(t + 1) * 512])])
                ln_rows(ln1_g[l], ln1_b[l], FP[full_index(p) - 1], 2 * TT)
                wq = peer_wq[l].rearrange("(k p) n -> p k n", p=P)
                for t in range(4):
                    wtile([(slot_view(KD, 512), wq[:, :, t * 512:(t + 1) * 512])])
                wtile([(slot_view(HEADS, P), peer_k1[l].rearrange("h n k -> n h k")),
                       (slot_view(HEADS, P, HEADS), peer_k2[l].rearrange("h n k -> n h k"))])
                ln_rows(ln2_g[l], ln2_b[l], p, TT)
                f = full_index(p)
                sp.wait_ge(R[p]["xs_dram"], R[p].at("xs_dram", 16 * TT))
                sp.wait_ge(R[p]["wo_s"], R[p].at("wo_s", 24))
                xv3 = xrows[f].rearrange("t q d -> q t d")
                with sp.Fori(0, NG) as i:
                    for h in range(2):
                        sp.wait_ge(xr_free, i * 2 + (f * 2 * NG + h + 1))
                        sp.dma_start(xr[:, h, :].rearrange("q (t d) -> q t d", t=GRP),
                                     xv3[:, bass.ds(i * (2 * GRP) + h * GRP, GRP), :]).then_inc(xr_land[h], 16)
                for h in range(2):
                    sp.wait_ge(y_out[h], 16 + 16 * NG * (f + 1))
                sp.dma_start(yrows[:, :, :], ysum[f].rearrange("(t p) d -> p t d", p=P)).then_inc(y_in, 16)
            sp.wait_ge(R[3]["x_new"], R[3].at("x_new", 2 * TT))
            sp.dma_start(out[0].rearrange("(t p) d -> p t d", p=P), X[:, 0]).then_inc(out_s, 16)
            sp.wait_ge(out_s, 16)

        @block.gpsimd
        def _(pool):
            nc.gpsimd.memset(um[:, :], 0.0).then_inc(set_up, 1)
            nc.gpsimd.memset(ones[:, :], 1.0 / 256.0).then_inc(set_up, 1)
            nc.gpsimd.memset(onesb[:, :], 1.0).then_inc(set_up, 1)
            nc.gpsimd.memset(eps[:, :], LN_EPS).then_inc(set_up, 1)
            nc.gpsimd.memset(hpad[:, :, :], 0.0).then_inc(set_up, 1)
            nc.gpsimd.memset(zcol[:, :, :, :], 0.0).then_inc(set_up, 1)
            for p in FP:
                f = full_index(p)
                l = PASSES[p][1]
                ut = (peer_u0, peer_u1)[l]
                vt = (peer_v0, peer_v1)[l]
                for tt in range(TT):
                    pool.wait_ge(R[p]["xsplit"], R[p].at("xsplit", tt + 1))
                    pool.dma_start(xrows[f, tt * P:(tt + 1) * P], xs[:, :, :]).then_inc(R[p]["xs_dram"], 16)
                pool.wait_ge(R[p]["sel_s"], R[p].at("sel_s", 2 * TT))
                pool.wait_ge(R[p]["sc_s"], R[p].at("sc_s", 4 * TT))

                def gather_u(i, h):
                    pool.wait_ge(u_free, i * (2 * GRP) + (f * TOK + (h + 1) * GRP))
                    pool.sem_inc(asked, 1)
                    nc.gpsimd.tensor_copy(eidx[:, 0, h, :], eT[:, bass.ds(i * (2 * GRP) + h * GRP, GRP)])\
                        .then_inc(u_staged, 1)
                    pool.wait_ge(u_staged, i * 2 + (f * 2 * NG + h + 1))
                    pool.sem_inc(asked, 1)
                    for k in range(GRP):
                        pool.indirect_dma_start(Ur[:, h * GRP + k, :], None, ut,
                                                bass.IndirectOffsetOnAxis(eidx[:, 0, h, k:k + 1], 0))\
                            .then_inc(u_land[h * GRP + k], 16)

                def gather_v(i, h):
                    pool.wait_ge(v_free, i * 2 + (f * 2 * NG + h + 1))
                    pool.sem_inc(asked, 1)
                    nc.gpsimd.tensor_copy(eidx[:, 1, h, :], eT[:, bass.ds(i * (2 * GRP) + h * GRP, GRP)])\
                        .then_inc(v_staged, 1)
                    pool.wait_ge(v_staged, i * 2 + (f * 2 * NG + h + 1))
                    pool.sem_inc(asked, 1)
                    for k in range(GRP):
                        pool.indirect_dma_start(Vr[:, h * GRP + k, :], None, vt,
                                                bass.IndirectOffsetOnAxis(eidx[:, 1, h, k:k + 1], 0))\
                            .then_inc(v_land[h * GRP + k], 16)

                for h in range(2):
                    gather_u(0, h)
                with pool.Fori(0, NG - 1) as i:
                    for h in range(2):
                        gather_v(i, h)
                        gather_u(i + 1, h)
                for h in range(2):
                    gather_v(NG - 1, h)

        @block.tensor
        def _(pe):
            wt = Weights()
            T = nc.tensor

            def arrived(dmas, turn=None, per=None):
                slot, v = wt.next(dmas)
                pe.wait_ge(w_land[slot], v if turn is None else turn * (16 * dmas) + v)
                return slot

            pe.sem_inc(w_used, 2)
            pe.sem_inc(v_free, 2)
            pe.sem_inc(xr_free, 2)
            pe.wait_ge(consts, 16 * 25)
            for q, n in enumerate([R_END, 2 * TAPS, R_END, 2 * TAPS, 16]):
                last = T.transpose(bank(q, 0, n), rows[0:n, q, :], ident[0:n, 0:n])
            last.then_inc(rows_t, 1)
            pe.wait_ge(set_up, 6)

            def echo(s):
                T.matmul(bank(7, 508, 510), onesb[:, :], onesb[:, 0:2], start=True, stop=True).then_inc(s, 1)

            def ada(l):
                pe.wait_ge(silu_s, 1)
                if l:
                    pe.wait_ge(R[1]["x_new"], R[1].at("x_new", 2 * TT))
                with pe.Fori(0, 6) as i:
                    for h in range(2):
                        s = arrived(1, i)
                        for j in range(4):
                            for k in range(KD):
                                last = T.matmul(PS[:, bass.ds(i * 16 + (7 * 512 + h * 8 + 2 * j), 2)],
                                                W[:, s, k * 512 + j * P:k * 512 + (j + 1) * P], silu_c[:, k, :],
                                                start=(k == 0), stop=(k == KD - 1))
                        last.then_inc(w_used, 1)
                wt.skip(10, 1)
                echo(mod_p)

            def transposes(p, src, a, ready, count, done):
                for tt in range(TT):
                    pe.wait_ge(R[p][ready], R[p].at(ready, count + tt + 1))
                    for k in range(KD):
                        last = T.transpose(bank(2 * tt + k // 4, (k % 4) * P, (k % 4 + 1) * P),
                                           src[:, tt, k * P:(k + 1) * P], ident[:, :])
                    last.then_inc(R[p][done], 1)

            def back(p, src, n, done):
                for tt in range(TT):
                    for k in range(KD):
                        last = T.transpose(bank(2 * tt + k // 4, (k % 4) * P, (k % 4 + 1) * P),
                                           src[:, k, tt * P:(tt + 1) * P], ident[:, :])
                    last.then_inc(R[p][done], 1)

            for p, (name, l, s, kv) in enumerate(PASSES):
                r = R[p]
                if p in (0, 2):
                    ada(l)
                transposes(p, scratch, 0, "xn", 0, "xnT")
                pe.wait_ge(r["u_ready"], r.at("u_ready", TT))
                units = units_of(s, kv)
                kinds = [u[0] in "TQ" for u in units]
                slot = None
                for n, (kind, tile, blk, dst) in enumerate(units):
                    if not n or units[n - 1][1] != tile:
                        slot = arrived(8 if kind == "Q" else 1)
                    if n >= 4:
                        m = n - 4
                        if kinds[m]:
                            pe.wait_ge(r["unit_act"], r.at("unit_act", sum(kinds[:m + 1])))
                        else:
                            pe.wait_ge(r["unit_dve"], r.at("unit_dve", m + 1 - sum(kinds[:m + 1])))
                    width = 256 if tile == 4 else 512
                    for k in range(KD):
                        wk = W[:, slot, k * width:(k + 1) * width]
                        go = dict(start=(k == 0), stop=(k == KD - 1))
                        if kind in "TQ":
                            last = T.matmul(bank(n % 4, 0, TOK), wk[:, blk * P:(blk + 1) * P], uT[:, k, :], **go)
                        elif kind == "N":
                            last = T.matmul(bank(n % 4), uT[:, k, dst * P:(dst + 1) * P], wk, **go)
                        else:
                            last = T.matmul(bank(n % 4, 0, P), uT[:, k, dst * P:(dst + 1) * P], wk[:, P:2 * P], **go)
                    last.then_inc(r["unit"], 1)
                    if n + 1 == len(units) or units[n + 1][1] != tile:
                        echo(w_used)
                if kv:
                    continue
                na = sum(kinds)
                nv = len(units) - na
                pe.wait_ge(r["unit_dve"], r.at("unit_dve", nv))
                pe.wait_ge(r["unit_act"], r.at("unit_act", na))
                for q in range(4):
                    cs, ct = q // 2, q % 2
                    for tt in range(TT):
                        last = T.matmul(bank(q, 0, TOK), nvf[s][:, tt, 2 * P + ct * P:2 * P + (ct + 1) * P],
                                        dft[:, tt, cs, :], start=(tt == 0), stop=(tt == TT - 1))
                    last.then_inc(r["unit"], 1)
                pe.wait_ge(r["unit_act"], r.at("unit_act", na + 4))
                for ct in range(2):
                    for cs in range(2):
                        last = T.matmul(bank(ct, 0, TOK), dftg[:, cs, :], fs[:, cs, ct, :],
                                        start=(cs == 0), stop=(cs == 1))
                    last.then_inc(r["unit"], 1)
                if s == 0:
                    for q in range(5):
                        last = T.matmul(PS[:, 4 * 512 + q * TOK:4 * 512 + (q + 1) * TOK], rot[:, :], gqk[:, q, :],
                                        start=True, stop=True)
                    last.then_inc(r["ropemm"], 1)
                    pe.wait_ge(r["roped"], r.at("roped", 1))
                jobs = attention_jobs()
                pe.wait_ge(r["unit_act"], r.at("unit_act", na + 6))

                def scores(n):
                    br, h, qt = jobs[n]
                    if n >= 2:
                        pe.wait_ge(r["sm"], r.at("sm", n - 1))
                    if br == 0:
                        o = (h % 2) * DH
                        q_ = nq[o:o + DH, h // 2, qt * P:(qt + 1) * P]
                        ks = [nkb[st][o:o + DH, h // 2, :] for st in ((0, 1) if s == 0 else (1,))]
                    else:
                        o = (h // 4) * DH
                        q_ = gqk[o:o + DH, h % 4, qt * P:(qt + 1) * P]
                        ks = [gqk[o:o + DH, 4, :], gkc[o:o + DH, :]] if s == 0 else [gkc[o:o + DH, :]]
                    for m, k_ in enumerate(ks):
                        last = T.matmul(bank(n % 2, m * TOK, (m + 1) * TOK), q_, k_, start=True, stop=True)
                    last.then_inc(r["S"], 1)

                def values(n):
                    br, h, qt = jobs[n]
                    nk = 4 if s == 0 else 2
                    pe.wait_ge(r["pn"], r.at("pn", n + 1))
                    if n >= 2:
                        pe.wait_ge(r["pts"], r.at("pts", n - 1))
                    for q in range(nk):
                        last = T.transpose(bank(2 + n % 2, q * P, (q + 1) * P), Pn[:, n % 2, q * P:(q + 1) * P],
                                           ident[:, :])
                    last.then_inc(r["ptp"], 1)
                    pe.wait_ge(r["pts"], r.at("pts", n + 1))
                    if n >= 2:
                        pe.wait_ge(r["y"], r.at("y", n - 1))
                    o = (h % 2) * DH
                    for q in range(nk):
                        st = (0, 0, 1, 1)[q] if s == 0 else 1
                        if br == 0:
                            v_ = nvf[st][:, q % 2, h * DH:(h + 1) * DH]
                        else:
                            v_ = gvb[st][:, q % 2, (h // 4) * DH:(h // 4 + 1) * DH]
                        last = T.matmul(PS[o:o + DH, (4 + n % 2) * 512:(4 + n % 2) * 512 + P], v_,
                                        PT[:, n % 2, q * P:(q + 1) * P], start=(q == 0), stop=(q == nk - 1))
                    last.then_inc(r["O"], 1)

                for n in range(len(jobs) + 1):
                    if n < len(jobs):
                        scores(n)
                    if n:
                        values(n - 1)
                pe.wait_ge(r["conv_done"], r.at("conv_done", 1))
                for q in range(2):
                    last = T.matmul(bank(6, 0, TOK), ones[:, :], hacc[:, q, :], start=(q == 0), stop=(q == 1))
                last.then_inc(r["cmean"], 1)
                pe.wait_ge(r["csq"], r.at("csq", 1))
                for q in range(2):
                    last = T.matmul(bank(6, TOK, 2 * TOK), ones[:, :], hsq[:, q, :], start=(q == 0), stop=(q == 1))
                last.then_inc(r["cvar"], 1)
                pe.wait_ge(r["y"], r.at("y", len(jobs)))
                pe.wait_ge(r["ya"], r.at("ya", 1))
                with pe.Fori(0, 4) as i:
                    for h in range(2):
                        s_ = arrived(8, i)
                        at = 32
                        for b, kt in enumerate((2, 2, 2, 4)):
                            pe.wait_ge(r["merged"], r.at("merged", i * 8 + (h * 4 + b + 1)))
                            for k in range(KD):
                                T.matmul(bank(b % 2, 0, TOK), W[:, s_, (k * NB + b) * P:(k * NB + b + 1) * P],
                                         uT[:, k, :], start=(k == 0), stop=(k == KD - 1))
                            for k in range(kt):
                                last = T.matmul(bank(b % 2, TOK, 2 * TOK), W[:, s_, (at + k) * P:(at + k + 1) * P],
                                                yb[:, at - 32 + k, :], start=(k == 0), stop=(k == kt - 1))
                            at += kt
                            last.then_inc(r["gate"], 1)
                        echo(w_used)
                wt.skip(6, 8)
                pe.wait_ge(r["macc"], r.at("macc", 8))

                def outT(n_tiles, src, done, copied, base):
                    for t in range(n_tiles):
                        s_ = arrived(1)
                        for j in range(4):
                            n = 4 * t + j
                            if n >= 4:
                                pe.wait_ge(r[copied], r.at(copied, base + n - 3))
                            for k in range(KD):
                                last = T.matmul(bank(n % 4, 0, TOK), W[:, s_, k * 512 + j * P:k * 512 + (j + 1) * P],
                                                src[:, k, :], start=(k == 0), stop=(k == KD - 1))
                            last.then_inc(r[done], 1)
                        echo(w_used)

                outT(2, mT, "wo", "wo_s", 0)
                pe.wait_ge(r["wo_s"], r.at("wo_s", 8))
                back(p, oT, 0, "resT")
                transposes(p, scratch, 0, "xn", TT, "xnT")
                pe.wait_ge(r["u_ready"], r.at("u_ready", 2 * TT))
                back(p, uT, 0, "urow")
                pe.wait_ge(r["xsplit"], r.at("xsplit", TT))
                outT(4, uT, "wo", "wo_s", 8)
                s_ = arrived(2)
                for q in range(SEG):
                    h, half = q // 2, q % 2
                    last = T.transpose(bank(4 + q // 4, (q % 4) * P, (q % 4 + 1) * P),
                                       W[:, s_, (half * HEADS + h) * P:(half * HEADS + h + 1) * P], ident[:, :])
                last.then_inc(r["keysT"], 1)
                pe.wait_ge(r["keys_s"], r.at("keys_s", 4))
                echo(w_used)
                pe.wait_ge(r["keys_s"], r.at("keys_s", 4))
                pe.wait_ge(r["wo_s"], r.at("wo_s", 8 + 16))
                for tt in range(TT):
                    for q in range(SEG):
                        if tt and q % 4 == 0:
                            pe.wait_ge(r["sc_s"], r.at("sc_s", q // 4 + 1))
                        last = T.matmul(bank(q // 4, (q % 4) * P, (q % 4 + 1) * P), qT[:, q, tt * P:(tt + 1) * P],
                                        kT[:, q, :], start=True, stop=True)
                        if q % 4 == 3:
                            last.then_inc(r["sc_ps"], 1)
                for tt in range(TT):
                    pe.wait_ge(r["sel"], r.at("sel", tt + 1))
                    if tt:
                        pe.wait_ge(r["sel_s"], r.at("sel_s", 2))
                    T.transpose(bank(4, 0, P), isel[:, 0, :], ident[:, :])
                    T.transpose(bank(4, P, 2 * P), ts[:, :, :].rearrange("p h k -> p (h k)"), ident[:, :])\
                        .then_inc(r["selT"], 1)
                pe.wait_ge(r["sel_s"], r.at("sel_s", 2 * TT))
                f = full_index(p)

                def broadcast(i, h, k):
                    if k == 0:
                        pe.wait_ge(xr_land[h], i * 16 + (f * NG * 16 + 16))
                    pe.wait_ge(u_free, i * (2 * GRP) + (f * TOK + h * GRP + k + RING - 1))
                    for q in range(2):
                        last = T.matmul(bank(2 * (k % 2) + q), ones3,
                                        xr[:, h, k * D + q * 512:k * D + (q + 1) * 512], start=True, stop=True)
                    last.then_inc(xb_s, 1)
                    if k == GRP - 1:
                        T.matmul(PS[96:128, 7 * 512 + 508:7 * 512 + 510], onesb[:, 0:32], onesb[:, 0:2],
                                 start=True, stop=True).then_inc(xr_free, 1)

                def weigh(i, h, k):
                    if k == 0:
                        pe.wait_ge(w_s, i * 2 + (f * 2 * NG + h + 1))
                        pe.wait_ge(yc_s, i * 2 + (f * 2 * NG + h + 1))
                    pe.wait_ge(v_land[h * GRP + k], i * 16 + (f * NG * 16 + 16))
                    for q in range(2):
                        last = T.matmul(PS[0:32, (4 + 2 * h + q) * 512:(5 + 2 * h + q) * 512], zcol[:, h, k, :],
                                        Vr[:, h * GRP + k, q * 512:(q + 1) * 512],
                                        start=(k == 0), stop=(k == GRP - 1))
                    if k == GRP - 1:
                        last.then_inc(v_free, 1)

                for h in range(2):
                    for k in range(GRP):
                        broadcast(0, h, k)
                with pe.Fori(0, NG - 1) as i:
                    for h in range(2):
                        for k in range(GRP):
                            weigh(i, h, k)
                            broadcast(i + 1, h, k)
                for h in range(2):
                    for k in range(GRP):
                        weigh(NG - 1, h, k)
                pe.wait_ge(r["g2"], 1)
                for k in range(KD):
                    last = T.matmul(bank(k // 4, (k % 4) * P, (k % 4 + 1) * P), mod[:, 40 + k, s:s + 1].to_broadcast([P, P]),
                                    ident[:, :], start=True, stop=True)
                last.then_inc(r["resT"], 1)

        @block.scalar
        def _(act):
            A = nc.scalar.activation
            act.sem_inc(yc_s, 2)
            act.sem_inc(y_out[0], 16)
            act.sem_inc(y_out[1], 16)
            act.wait_ge(cols_s, 1)
            A(silu_c[:, :, :].rearrange("p k s -> p s k"), cols[:, 4, 0:16].rearrange("p (s k) -> p s k", s=2),
              ACT.Silu).then_inc(silu_s, 1)
            act.wait_ge(set_up, 6)

            def spread(p, stat, std, count):
                act.wait_ge(R[p][stat], R[p].at(stat, count))
                A(sd[:, 0:1], mv[:, 1:2], ACT.Sqrt, bias=eps[:, 0:1]).then_inc(R[p][std], 1)

            def modulate(p, s, base, shift, scale):
                r = R[p]
                for tt in range(TT):
                    spread(p, "stat", "std", base + tt + 1)
                for tt in range(TT):
                    act.wait_ge(r["xnT"], r.at("xnT", base + tt + 1))
                    for k in range(KD):
                        last = A(uT[:, k, tt * P:(tt + 1) * P], bank(2 * tt + k // 4, (k % 4) * P, (k % 4 + 1) * P),
                                 ACT.Identity, scale=mod[:, scale + k, s:s + 1], bias=mod[:, shift + k, s:s + 1])
                    last.then_inc(r["u_ready"], 1)

            for p, (name, l, s, kv) in enumerate(PASSES):
                r = R[p]
                a = 2 * l
                act.wait_ge(mod_s, l + 1)
                modulate(p, s, 0, 0, 8)
                dst_of = {"cv": lambda j: cv[:, j, :], "nq": lambda j: nq[:, j, :], "nk": lambda j: nkb[s][:, j, :],
                          "gq": lambda j: gqk[:, j, :], "gk": lambda j: gqk[:, 4, :] if s == 0 else gkc[:, :]}
                units = units_of(s, kv)
                for n, (kind, tile, blk, dst) in enumerate(units):
                    if kind in "TQ":
                        col = R_GQ + blk if kind == "Q" else 4 * tile + blk
                        act.wait_ge(r["unit"], r.at("unit", n + 1))
                        fn = ACT.Sigmoid if dst[0] == "cv" and dst[1] >= 2 else ACT.Identity
                        A(dst_of[dst[0]](dst[1]), bank(n % 4, 0, TOK), fn, bias=cols[:, a, col:col + 1])\
                            .then_inc(r["unit_act"], 1)
                if kv:
                    continue
                nu = len(units)
                for q in range(4):
                    act.wait_ge(r["unit"], r.at("unit", nu + q + 1))
                    A(fs[:, q // 2, q % 2, :], bank(q, 0, TOK), ACT.Copy).then_inc(r["unit_act"], 1)
                for q in range(2):
                    act.wait_ge(r["unit"], r.at("unit", nu + 4 + q + 1))
                    A(yb[:, 4 + q, :], bank(q, 0, TOK), ACT.Copy).then_inc(r["unit_act"], 1)
                jobs = attention_jobs()
                w = 2 * TOK if s == 0 else TOK

                def exps(n):
                    br, h, qt = jobs[n]
                    q = n % 2
                    act.wait_ge(r["sm"], r.at("sm", n + 1))
                    if n >= 2:
                        act.wait_ge(r["ptp"], r.at("ptp", n - 1))
                    last = A(Pn[:, q, 0:w], Sm[:, q, 0:w], ACT.Exp, bias=st8[:, q, 1:2], accum_out=st8[:, q, 2:3])
                    if br:
                        last = A(st8[:, q, 3:4], sink[:, h:h + 1], ACT.Exp, bias=st8[:, q, 1:2])
                    last.then_inc(r["exp"], 1)

                def copies(n):
                    br, h, qt = jobs[n]
                    q = n % 2
                    act.wait_ge(r["ptp"], r.at("ptp", n + 1))
                    A(PT[:, q, 0:w], bank(2 + q, 0, w), ACT.Copy).then_inc(r["pts"], 1)
                    act.wait_ge(r["O"], r.at("O", n + 1))
                    o = (h % 2) * DH
                    A(yb[o:o + DH, (2, 6)[br] + h // 2, qt * P:(qt + 1) * P],
                      PS[o:o + DH, (4 + q) * 512:(4 + q) * 512 + P], ACT.Copy).then_inc(r["y"], 1)

                for n in range(len(jobs) + 1):
                    if n < len(jobs):
                        exps(n)
                    if n:
                        copies(n - 1)
                act.wait_ge(r["cvar"], r.at("cvar", 1))
                A(hstd[:, :], bank(6, TOK, 2 * TOK), ACT.Sqrt, bias=eps[:, 0:1]).then_inc(r["cstd"], 1)
                act.wait_ge(r["cnorm"], r.at("cnorm", 1))
                for q in range(2):
                    last = A(yb[:, q, :], hacc[:, q, :], ACT.Silu, scale=cols[:, a, R_CG + q:R_CG + q + 1],
                             bias=cols[:, a, R_CLB + q:R_CLB + q + 1])
                last.then_inc(r["ya"], 1)
                with act.Fori(0, 4) as i:
                    for h in range(2):
                        for b in range(NB):
                            act.wait_ge(r["gate"], r.at("gate", i * 8 + (h * 4 + b + 1)))
                            A(sg[:, b % 2, :], bank(b % 2, 0, TOK), ACT.Sigmoid,
                              bias=cols[:, a, bass.ds(i * 2 + (C_GATE + b * KD + h), 1)]).then_inc(r["sig"], 1)
                for n in range(KD):
                    act.wait_ge(r["wo"], r.at("wo", n + 1))
                    A(oT[:, n, :], bank(n % 4, 0, TOK), ACT.Copy, scale=mod[:, 16 + n, s:s + 1])\
                        .then_inc(r["wo_s"], 1)
                for tt in range(TT):
                    spread(p, "rstat", "rstd", tt + 1)
                modulate(p, s, TT, 24, 32)
                for n in range(SEG):
                    act.wait_ge(r["wo"], r.at("wo", 8 + n + 1))
                    A(qT[:, n, :], bank(n % 4, 0, TOK), ACT.Copy).then_inc(r["wo_s"], 1)
                act.wait_ge(r["keysT"], r.at("keysT", 1))
                for q in range(4):
                    A(kT[:, 4 * q:4 * q + 4, :].rearrange("p a n -> p (a n)"), bank(4 + q), ACT.Copy)\
                        .then_inc(r["keys_s"], 1)
                for tt in range(TT):
                    if tt:
                        act.wait_ge(r["tsub"], r.at("tsub", tt))
                    for q in range(4):
                        act.wait_ge(r["sc_ps"], r.at("sc_ps", 4 * tt + q + 1))
                        A(big[0][:, q * 512:(q + 1) * 512], bank(q), ACT.Copy).then_inc(r["sc_s"], 1)
                    act.wait_ge(r["tsub"], r.at("tsub", tt + 1))
                    A(ts[:, :, :], ts[:, :, :], ACT.Exp).then_inc(r["texp"], 1)
                    act.wait_ge(r["selT"], r.at("selT", tt + 1))
                    A(eT[:, tt * P:(tt + 1) * P], bank(4, 0, P), ACT.Copy).then_inc(r["sel_s"], 1)
                    A(gT[:, tt * P:(tt + 1) * P], bank(4, P, 2 * P), ACT.Copy).then_inc(r["sel_s"], 1)
                f = full_index(p)

                def gelu(i, h):
                    act.wait_ge(u_free, i * (2 * GRP) + (f * TOK + (h + 1) * GRP + RING))
                    A(ge[:, h, :], hcol[:, h, :], ACT.Gelu).then_inc(gelu_s, 1)

                def put_sums(i, h):
                    act.wait_ge(v_free, i * 2 + (f * 2 * NG + h + 3))
                    act.wait_ge(y_out[h], i * 16 + (f * NG * 16 + 16))
                    A(ystage[:, h, :], PS[0:GRP, (4 + 2 * h) * 512:(6 + 2 * h) * 512], ACT.Copy).then_inc(yc_s, 1)
                    act.wait_ge(yc_s, i * 2 + (f * 2 * NG + h + 3))
                    act.dma_start(ysum[f, bass.ds(i * (2 * GRP) + h * GRP, GRP), :], ystage[:, h, :])\
                        .then_inc(y_out[h], 16)

                for h in range(2):
                    gelu(0, h)
                with act.Fori(0, NG - 1) as i:
                    for h in range(2):
                        put_sums(i, h)
                        gelu(i + 1, h)
                for h in range(2):
                    put_sums(NG - 1, h)
                for tt in range(TT):
                    spread(p, "rstat", "rstd", TT + tt + 1)

        @block.vector
        def _(dve):
            V = nc.vector
            ch = Chain(dve, dch_s)
            scr = scratch[:, :, :].rearrange("p t d -> p (t d)")
            dve.sem_inc(u_free, RING)
            dve.wait_ge(rows_t, 1)
            for q, n in enumerate([R_END, 2 * TAPS, R_END, 2 * TAPS, 16]):
                last = V.tensor_copy(cols[:, q, 0:n], bank(q, 0, n))
            last.then_inc(cols_s, 1)
            dve.wait_ge(cols_s, 1)

            def stats(src, inc):
                for q in range(2):
                    ch.add(V.bn_stats(bst[:, q, :], src[:, q * 512:(q + 1) * 512]))
                ch.wait()
                V.bn_aggr(mv[:, :], bst[:, :, :]).then_inc(inc, 1)

            def norm(dst, src, std, count, inc=None):
                dve.wait_ge(std, count)
                ch.link(V.reciprocal(sd[:, 1:2], sd[:, 0:1]))
                ins = V.tensor_scalar(dst, src, mv[:, 0:1], sd[:, 1:2], ALU.subtract, ALU.mult)
                if inc is None:
                    ch.link(ins)
                else:
                    ins.then_inc(inc, 1)

            def norm_rows(p, s, base):
                r = R[p]
                for tt in range(TT):
                    stats(X[:, s, tt, :], r["stat"])
                    norm(scratch[:, tt, :], X[:, s, tt, :], r["std"], r.at("std", base + tt + 1), r["xn"])

            ln = [0]

            def residual(p, s, base):
                r = R[p]
                ln[0] += 1
                dve.wait_ge(ln_land, 32 * ln[0])
                for tt in range(TT):
                    if base:
                        add = yrows[:, tt, :]
                    else:
                        dve.wait_ge(r["resT"], r.at("resT", tt + 1))
                        add = PS[:, tt * D:(tt + 1) * D]
                    ch.link(V.scalar_tensor_tensor(scratch[:, tt, :], X[:, s, tt, :], ALPHA, add, ALU.mult, ALU.add))
                    stats(scratch[:, tt, :], r["rstat"])
                    norm(scratch[:, tt, :], scratch[:, tt, :], r["rstd"], r.at("rstd", base + tt + 1))
                    ch.link(V.tensor_tensor(scratch[:, tt, :], scratch[:, tt, :], lnrow[:, 0, :], ALU.mult))
                    V.tensor_tensor(X[:, s, tt, :], scratch[:, tt, :], lnrow[:, 1, :], ALU.add).then_inc(r["x_new"], 1)
                    dve.wait_ge(r["x_new"], r.at("x_new", base + tt + 1))

            for p, (name, l, s, kv) in enumerate(PASSES):
                r = R[p]
                a = 2 * l
                if p in (0, 2):
                    dve.wait_ge(mod_p, l + 1)
                    badd = cols[:, a, R_ADA:R_CB].unsqueeze(2).to_broadcast([P, 48, 2])
                    ch.link(V.tensor_tensor(mod[:, :, :], bank(7, 0, 96).rearrange("p (n s) -> p n s", s=2), badd, ALU.add))
                    for q in (8, 32):
                        ch.link(V.tensor_scalar_add(mod[:, q:q + 8, :], mod[:, q:q + 8, :], 1.0))
                    dve.sem_inc(mod_s, 1)
                    dve.wait_ge(bias_s, 16 * ROWS * NAT_H * (l + 1))
                    for tt in range(TT):
                        ch.add(V.tensor_tensor(bias[:, tt, :, :], bias[:, tt, :, :],
                                               masks[:, tt, 0:1, :].to_broadcast([P, NAT_H, TOK]), ALU.add))
                    ch.wait()
                    dve.wait_ge(lrow_s, 48 * (l + 1))
                norm_rows(p, s, 0)
                units = units_of(s, kv)
                for n, (kind, tile, blk, dst) in enumerate(units):
                    if kind == "N":
                        dve.wait_ge(r["unit"], r.at("unit", n + 1))
                        V.tensor_tensor(nvf[s][:, dst, :], bank(n % 4), brow[:, 0:4 * P], ALU.add)\
                            .then_inc(r["unit_dve"], 1)
                    elif kind == "V":
                        dve.wait_ge(r["unit"], r.at("unit", n + 1))
                        V.tensor_tensor(gvb[s][:, dst, :], bank(n % 4, 0, P), brow[:, 4 * P:5 * P], ALU.add)\
                            .then_inc(r["unit_dve"], 1)
                if kv:
                    continue
                na = sum(u[0] in "TQ" for u in units)
                if s == 0:
                    dve.wait_ge(r["ropemm"], r.at("ropemm", 1))
                    t5 = scr[:, 0:5 * TOK].rearrange("p (q t) -> p q t", q=5)
                    ch.add(V.tensor_tensor(t5, PS[:, 4 * 512:4 * 512 + 5 * TOK].rearrange("p (q t) -> p q t", q=5),
                                           rope[:, 1:2, :].to_broadcast([P, 5, TOK]), ALU.mult))
                    ch.link(V.tensor_tensor(gqk[:, :, :], gqk[:, :, :], rope[:, 0:1, :].to_broadcast([P, 5, TOK]),
                                            ALU.mult))
                    V.tensor_tensor(gqk[:, :, :], gqk[:, :, :], t5, ALU.add).then_inc(r["roped"], 1)
                jobs = attention_jobs()
                w = 2 * TOK if s == 0 else TOK

                def scaled(n):
                    br, h, qt = jobs[n]
                    q = n % 2
                    dve.wait_ge(r["S"], r.at("S", n + 1))
                    if s == 0:
                        m_ = bias[:, qt, h, :] if br == 0 else masks[:, qt, 1, :]
                        ch.add(V.scalar_tensor_tensor(Sm[:, q, 0:TOK], bank(q, 0, TOK), SCALE, m_, ALU.mult, ALU.add))
                        ch.link(V.tensor_scalar(Sm[:, q, TOK:w], bank(q, TOK, w), SCALE, None, ALU.mult))
                    else:
                        ch.link(V.tensor_scalar(Sm[:, q, 0:w], bank(q, 0, w), SCALE, None, ALU.mult))
                    ch.link(V.reduce_max(st8[:, q, 0:1], Sm[:, q, 0:w], AX))
                    if br:
                        ch.link(V.tensor_tensor(st8[:, q, 0:1], st8[:, q, 0:1], sink[:, h:h + 1], ALU.max))
                    V.tensor_scalar(st8[:, q, 1:2], st8[:, q, 0:1], -1.0, None, ALU.mult).then_inc(r["sm"], 1)

                def normed(n):
                    br, h, qt = jobs[n]
                    q = n % 2
                    dve.wait_ge(r["exp"], r.at("exp", n + 1))
                    if br:
                        ch.link(V.tensor_tensor(st8[:, q, 2:3], st8[:, q, 2:3], st8[:, q, 3:4], ALU.add))
                    ch.link(V.reciprocal(st8[:, q, 4:5], st8[:, q, 2:3]))
                    V.tensor_scalar(Pn[:, q, 0:w], Pn[:, q, 0:w], st8[:, q, 4:5], None, ALU.mult).then_inc(r["pn"], 1)

                for n in range(len(jobs) + 1):
                    if n < len(jobs):
                        scaled(n)
                    if n:
                        normed(n - 1)
                dve.wait_ge(set_up, 6)
                dve.wait_ge(r["unit_act"], r.at("unit_act", 4))
                half = TAPS // 2
                ch.link(V.tensor_tensor(hpad[:, :, half:half + TOK], cv[:, 0:2, :], cv[:, 2:4, :], ALU.mult))
                for t in range(TAPS):
                    for q in range(2):
                        tap = cols[:, a + 1, 2 * t + q:2 * t + q + 1]
                        if t == 0:
                            ins = V.tensor_scalar(hacc[:, q, :], hpad[:, q, 0:TOK], tap,
                                                  cols[:, a, R_CB + q:R_CB + q + 1], ALU.mult, ALU.add)
                        else:
                            ins = V.scalar_tensor_tensor(hacc[:, q, :], hpad[:, q, t:t + TOK], tap, hacc[:, q, :],
                                                         ALU.mult, ALU.add)
                        if t == TAPS - 1 and q == 1:
                            ins.then_inc(r["conv_done"], 1)
                        else:
                            ch.add(ins)
                    if t < TAPS - 1:
                        ch.wait()
                dve.wait_ge(r["cmean"], r.at("cmean", 1))
                ch.link(V.tensor_tensor(hacc[:, :, :], hacc[:, :, :],
                                        bank(6, 0, TOK).unsqueeze(1).to_broadcast([P, 2, TOK]), ALU.subtract))
                V.tensor_tensor(hsq[:, :, :], hacc[:, :, :], hacc[:, :, :], ALU.mult).then_inc(r["csq"], 1)
                dve.wait_ge(r["cstd"], r.at("cstd", 1))
                ch.link(V.reciprocal(hstd[:, :], hstd[:, :]))
                V.tensor_tensor(hacc[:, :, :], hacc[:, :, :], hstd[:, :].unsqueeze(1).to_broadcast([P, 2, TOK]),
                                ALU.mult).then_inc(r["cnorm"], 1)
                dve.sem_inc(r["merged"], 2)
                with dve.Fori(0, 4) as i:
                    ch.loop(i, 4)
                    for h in range(2):
                        mrow = mT[:, bass.ds(i * 2 + h, 1), :].rearrange("p a t -> p (a t)")
                        for b in range(NB):
                            dve.wait_ge(r["sig"], r.at("sig", i * 8 + (h * 4 + b + 1)))
                            to = mrow if b == 0 else prod[:, b % 2, :]
                            V.tensor_tensor(to, sg[:, b % 2, :], bank(b % 2, TOK, 2 * TOK), ALU.mult)\
                                .then_inc(r["merged"], 1)
                            dve.wait_ge(r["merged"], r.at("merged", i * 8 + (h * 4 + b + 3)))
                            if b:
                                ins = V.tensor_tensor(mrow, mrow, prod[:, b % 2, :], ALU.add)
                                if b == NB - 1:
                                    ins.then_inc(r["macc"], 1)
                                else:
                                    ch.link(ins)
                ch.end(4)
                residual(p, s, 0)
                norm_rows(p, s, TT)
                for tt in range(TT):
                    rows_ = PS[:, tt * 1024:(tt + 1) * 1024]
                    dve.wait_ge(r["urow"], r.at("urow", tt + 1))
                    if tt:
                        dve.wait_ge(r["xs_dram"], r.at("xs_dram", 16 * tt))
                    ch.link(V.tensor_copy(xs[:, 0, :], rows_))
                    ch.link(V.tensor_tensor(scratch[:, tt, :], rows_, xs[:, 0, :], ALU.subtract))
                    ch.link(V.tensor_copy(xs[:, 1, :], scratch[:, tt, :]))
                    ch.link(V.tensor_tensor(scratch[:, tt, :], scratch[:, tt, :], xs[:, 1, :], ALU.subtract))
                    V.tensor_copy(xs[:, 2, :], scratch[:, tt, :]).then_inc(r["xsplit"], 1)

                def top16(vals, idx, src, spare, segs):
                    for g in range(segs):
                        ch.add(V.max(vals[:, g, 0:8], src[:, g, :]))
                    ch.wait()
                    for g in range(segs):
                        ch.add(V.max_index(idx[:, g, 0:8], vals[:, g, 0:8], src[:, g, :]))
                        ch.add(V.match_replace(spare[:, g, :], vals[:, g, 0:8], src[:, g, :], LOWEST))
                    ch.wait()
                    for g in range(segs):
                        ch.add(V.max(vals[:, g, 8:16], spare[:, g, :]))
                    ch.wait()
                    for g in range(segs):
                        ch.add(V.max_index(idx[:, g, 8:16], vals[:, g, 8:16], spare[:, g, :]))
                    ch.wait()

                for tt in range(TT):
                    dve.wait_ge(r["sc_s"], r.at("sc_s", 4 * tt + 4))
                    if tt:
                        dve.wait_ge(r["sel_s"], r.at("sel_s", 2 * tt))
                    seg = [big[q].rearrange("p (g n) -> p g n", g=SEG) for q in range(2)]
                    top16(v16, i16, seg[0], seg[1], SEG)
                    ch.add(V.tensor_copy(i16f[:, :, :], i16[:, :, :]))
                    vv = v16[:, :, :].rearrange("p (h e) k -> p h e k", e=2)
                    iv = i16f[:, :, :].rearrange("p (h e) k -> p h e k", e=2)
                    cand = big[2].rearrange("p (h a b) -> p h a b", h=HEADS, a=TOPK)
                    full = [P, HEADS, TOPK, TOPK]
                    ch.link(V.tensor_tensor(cand, vv[:, :, 0, :].unsqueeze(3).to_broadcast(full),
                                            vv[:, :, 1, :].unsqueeze(2).to_broadcast(full), ALU.add))
                    c8 = [big[q].rearrange("p (g n) -> p g n", g=HEADS) for q in (2, 1)]
                    top16(ts, pos, c8[0], c8[1], HEADS)
                    posf = pos[:, :, :].rearrange("p h k -> p (h k)")
                    ch.add(V.tensor_single_scalar(ab[:, 0, :], posf, 4, ALU.logical_shift_right))
                    ch.link(V.tensor_single_scalar(ab[:, 1, :], posf, 15, ALU.bitwise_and))
                    ch.link(V.tensor_copy(abf[:, :, :], ab[:, :, :]))
                    one = big[3].rearrange("p (m a) -> p m a", a=TOPK)
                    one4 = big[3].rearrange("p (h k a) -> p h k a", h=HEADS, k=TOPK)
                    for e in range(2):
                        ch.link(V.tensor_tensor(one, abf[:, e, :].unsqueeze(2).to_broadcast([P, P, TOPK]),
                                                iota[:, :].unsqueeze(1).to_broadcast([P, P, TOPK]), ALU.is_equal))
                        ch.link(V.tensor_tensor(one4, one4, iv[:, :, e, :].unsqueeze(2).to_broadcast(full), ALU.mult))
                        ch.link(V.reduce_sum(isel[:, e, :], one, AX))
                    ch.link(V.scalar_tensor_tensor(isel[:, 0, :], isel[:, 0, :], float(NKEY), isel[:, 1, :],
                                                   ALU.mult, ALU.add))
                    ch.link(V.tensor_copy(hsum[:, 0, :], ts[:, :, 0:1].rearrange("p h k -> p (h k)")))
                    top = [P, HEADS, TOPK]
                    V.tensor_tensor(ts[:, :, :], ts[:, :, :], hsum[:, 0, :].unsqueeze(2).to_broadcast(top),
                                    ALU.subtract).then_inc(r["tsub"], 1)
                    dve.wait_ge(r["texp"], r.at("texp", tt + 1))
                    ch.link(V.reduce_sum(hsum[:, 1, :], ts[:, :, :], AX))
                    ch.link(V.reciprocal(hsum[:, 1, :], hsum[:, 1, :]))
                    V.tensor_tensor(ts[:, :, :], ts[:, :, :], hsum[:, 1, :].unsqueeze(2).to_broadcast(top),
                                    ALU.mult).then_inc(r["sel"], 1)
                f = full_index(p)
                dve.wait_ge(r["sel_s"], r.at("sel_s", 2 * TT))
                with dve.Fori(0, NG) as i:
                    for h in range(2):
                        for k in range(GRP):
                            dve.wait_ge(xb_s, i * (2 * GRP) + (f * TOK + h * GRP + k + 1))
                            dve.wait_ge(u_land[h * GRP + k], i * 16 + (f * NG * 16 + 16))
                            V.tensor_tensor_reduce(out=junk, in0=Ur[:, h * GRP + k, :],
                                                   in1=PS[:, (k % 2) * 1024:(k % 2 + 1) * 1024], scale=1.0, scalar=0.0,
                                                   op0=ALU.mult, op1=ALU.add, accum_out=hcol[:, h, k:k + 1])\
                                .then_inc(u_free, 1)
                            dve.wait_ge(u_free, i * (2 * GRP) + (f * TOK + h * GRP + k + 1 + RING))
                        dve.wait_ge(gelu_s, i * 2 + (f * 2 * NG + h + 1))
                        dve.wait_ge(v_free, i * 2 + (f * 2 * NG + h + 1))
                        V.tensor_tensor(zcol[:, h, :, :].rearrange("p a b -> p (a b)")[:, 0:(GRP - 1) * 33 + 1:33], ge[:, h, :], gT[:, bass.ds(i * (2 * GRP) + h * GRP, GRP)],
                                        ALU.mult).then_inc(w_s, 1)
                dve.wait_ge(yc_s, 2 + 2 * NG * (f + 1))
                dve.sem_inc(r["g2"], 1)
                dve.wait_ge(r["resT"], r.at("resT", TT + 1))
                dve.wait_ge(y_in, 16 * (f + 1))
                for tt in range(TT):
                    ins = V.tensor_tensor(yrows[:, tt, :], yrows[:, tt, :], PS[:, 0:D], ALU.mult)
                    ch.link(ins)
                residual(p, s, TT)


INPUTS = ["x", "c", "ctx", "c_ctx", "w_ada", "b_ada", "w_in", "b_in", "conv_w", "conv_b", "conv_ln_g", "conv_ln_b",
          "nat_rpb", "gqa_sink", "w_branch_a", "w_branch_b", "w_branch_c", "w_branch_d", "w_out", "ln1_g", "ln1_b",
          "peer_wq", "peer_k1", "peer_k2", "ln2_g", "ln2_b"]


def shape_constants():
    import numpy as np
    f = np.float32
    t = np.arange(TOK)
    w = 2 * np.pi * ((t[:, None] * t[None, :]) % TOK) / TOK
    both = np.stack([np.cos(w), np.sin(w)])
    dft = both.reshape(2, TT, P, TOK).transpose(2, 1, 0, 3)
    g = np.arange(DH)
    v = 2 * np.pi * ((g[:, None] * g[None, :]) % DH) / DH
    norm = 1.0 / np.sqrt(TOK * DH)
    dftg = np.zeros((P, 2, P))
    for q in range(2):
        sl = slice(q * DH, (q + 1) * DH)
        dftg[sl, 0, sl] = np.cos(v) * norm
        dftg[sl, 1, sl] = -np.sin(v) * norm
    quarter = DH // 4
    freqs = f(10000.0) ** (-np.arange(quarter, dtype=f) / f(quarter))
    rope = np.zeros((P, 2, TOK), f)
    rot = np.zeros((P, P), f)
    for m in range(P):
        d = m % DH
        ang = ((t // GRID_W) if d < DH // 2 else (t % GRID_W)).astype(f) * freqs[d % quarter]
        rope[m, 0] = np.cos(ang)
        rope[m, 1] = np.sin(ang)
        first = (d % (DH // 2)) < quarter
        if first:
            rot[m + quarter, m] = -1.0
        else:
            rot[m - quarter, m] = 1.0
    col = np.arange(GRID_W)
    start = np.clip(col - 8, 0, GRID_W - 16)
    inside = (col[None, :] >= start[:, None]) & (col[None, :] < start[:, None] + 16)
    nat = np.where(np.tile(inside, (ROWS, ROWS)), 0.0, -1e30)
    band = np.where(np.abs(t[:, None] - t[None, :]) <= 128, 0.0, -1e30)
    masks = np.stack([nat, band]).reshape(2, TT, P, TOK).transpose(2, 1, 0, 3)
    iota = np.tile(np.arange(TOPK), (P, 1))
    out = dict(ident_c=np.eye(P), dft_c=dft, dftg_c=dftg, rope_c=rope, rot_c=rot, mask_c=masks, iota_c=iota)
    return {k: np.ascontiguousarray(a).astype(f) for k, a in out.items()}


def kernel(**inputs):
    import numpy as np
    import concourse.bacc as bacc
    from concourse.bass_utils import run_bass_kernel_spmd

    nc = bacc.Bacc("TRN2", target_bir_lowering=False, num_devices=1)
    arrays = {n: np.ascontiguousarray(inputs[n]) for n in INPUTS}
    arrays.update(shape_constants())
    for n in ("peer_u", "peer_v"):
        for l in range(DEPTH):
            arrays[f"{n}{l}"] = np.ascontiguousarray(inputs[n][l])
    args = {}
    for n, a in arrays.items():
        args[n] = nc.dram_tensor("in_" + n, a.shape, mybir.dt.from_np(a.dtype), kind="ExternalInput").ap()
    out = nc.dram_tensor("out_x", (1, TOK, D), F32, kind="ExternalOutput").ap()
    build(nc, out=out, **args)
    r = run_bass_kernel_spmd(nc, [{"in_" + n: a for n, a in arrays.items()}], core_ids=[0])
    return r.results[0]["out_x"]
```

```python
import concourse.bass as bass
from concourse import mybir
from contextlib import ExitStack

F32 = mybir.dt.float32
F32R = mybir.dt.float32r
BF16 = mybir.dt.bfloat16
U32 = mybir.dt.uint32
ALU = mybir.AluOpType
ACT = mybir.ActivationFunctionType
AX = mybir.AxisListType.X

D = 1024
P = 128
TOK = 256
TT = TOK // P
KD = D // P
DEPTH = 2
GRID_W = 64
ROWS = TOK // GRID_W
TAPS = 31
DH = 64
NAT_H, GQA_H = 4, 8
RPB_W = 31
BANDS = 2 * ROWS - 1
PADW = 96
NAT_DR = 15
NB = 4
HEADS, TOPK, NKEY = 8, 16, 128
SEG = 2 * HEADS
PAIR_B, PAIR_C = TOPK, TOPK + 7 * 8
PAIRS = PAIR_C + 8
LN_EPS = 1e-5
ALPHA = (2 * DEPTH) ** 0.25
SCALE = DH ** -0.5
LOWEST = -3.0e38
C_NQ, C_NV, C_GQ, C_GK, C_GV, C_GATE = 4, 8, 12, 16, 17, 18
R_ADA, R_CB, R_CG, R_CLB, R_GQ, R_END = 50, 98, 100, 102, 104, 108
GRP = 4
RING = 8
SBANK = (0, 1, 6)
WBLK = 42

PASSES = [("ctx0", 0, 1, False), ("lat0", 0, 0, False), ("kv1", 1, 1, True), ("lat1", 1, 0, False)]


class Weights:

    def __init__(self):
        self.n = 0
        self.landed = [0, 0]

    def next(self, dmas):
        slot = self.n % 2
        self.n += 1
        self.landed[slot] += 16 * dmas
        return slot, self.landed[slot]

    def skip(self, tiles, dmas):
        for _ in range(tiles):
            self.next(dmas)


def merge_tiles(p):
    wt = Weights()
    wt.skip(12, 1)
    for q, (name, l, s, kv) in enumerate(PASSES):
        if kv:
            wt.skip(3, 1)
            continue
        wt.skip(3, 1)
        wt.skip(1, 8)
        wt.skip(1, 1)
        if q == p:
            return [wt.next(8), wt.next(8)]
        wt.skip(8, 8)
        wt.skip(2, 1)
        wt.skip(1, 2)
        wt.skip(4, 1)
        if q == 1:
            wt.skip(12, 1)


def merge_steps():
    for h in range(2):
        for b in range(NB):
            n = h * NB + b + 2
            yield h, b, (n // (2 * NB), n // NB % 2, n % NB)


class Chain:

    def __init__(self, eng, sem):
        self.eng, self.sem, self.n, self.off = eng, sem, 0, None

    def add(self, ins):
        self.n += 1
        ins.then_inc(self.sem, 1)
        return ins

    def wait(self):
        self.eng.wait_ge(self.sem, self.n if self.off is None else self.off + self.n)

    def link(self, ins):
        self.add(ins)
        self.wait()

    def loop(self, i, per):
        self.off, self.per, self.at = i * per, per, self.n

    def end(self, turns):
        assert self.n - self.at == self.per, (self.n, self.at, self.per)
        self.n += self.per * (turns - 1)
        self.off = None


def units_of(stream, kv):
    if kv:
        return [("T", 1, 2, ("nk", 0)), ("T", 1, 3, ("nk", 1)), ("N", 2, 0, 0), ("N", 2, 0, 1),
                ("T", 4, 0, ("gk", 0)), ("V", 4, 1, 0), ("V", 4, 1, 1)]
    u = [("T", 0, j, ("cv", j)) for j in range(4)]
    u += [("T", 1, j, (("nq", "nk")[j // 2], j % 2)) for j in range(4)]
    u += [("N", 2, 0, 0), ("N", 2, 0, 1)]
    u += [("Q", 3, j, ("gq", j)) for j in range(4)]
    u += [("T", 4, 0, ("gk", 0)), ("V", 4, 1, 0), ("V", 4, 1, 1)]
    return u


def attention_jobs():
    return [(br, h, qt) for br, heads in ((0, NAT_H), (1, GQA_H)) for h in range(heads) for qt in range(TT)]


def build(nc, x, c, ctx, c_ctx, w_ada, b_ada, w_in, b_in, conv_w, conv_b, conv_ln_g, conv_ln_b, nat_rpb,
          gqa_sink, w_branch_a, w_branch_b, w_branch_c, w_branch_d, w_out, ln1_g, ln1_b, peer_wq, peer_k1,
          peer_k2, peer_u0, peer_u1, peer_v0, peer_v1, ln2_g, ln2_b, ident_c, dft_c, dftg_c, rope_c, rot_c, mask_c, iota_c, out):
    es = ExitStack()
    with es:
        def sb(name, shape, dt=F32):
            return es.enter_context(nc.sbuf_tensor(name, shape, dt))

        def sem(name):
            return es.enter_context(nc.semaphore(name))

        with nc.sbuf_tensor("split", [P, 2 * RING * D], F32R) as split:
            pass
        arena = sb("arena", [P, 2 * RING * D])
        um = sb("um", [P, 2 * KD * TOK])

        def part(at, shape, dt=F32, of=arena):
            n = 1
            for d_ in shape:
                n *= d_
            v = of[:, at:at + n]
            if dt != F32 and dt != F32R:
                v = v.bitcast(dt)
            if len(shape) == 2:
                v = v.rearrange("p (a b) -> p a b", a=shape[0])
            elif len(shape) == 3:
                v = v.rearrange("p (a b c) -> p a b c", a=shape[0], b=shape[1])
            return v, at + n

        X = sb("X", [P, 2, TT, D])
        scratch = sb("scratch", [P, TT, D])
        oT = sb("oT", [P, KD, TOK])
        W = sb("W", [P, 2, WBLK * P])
        ident = sb("ident", [P, P])
        dft = sb("dft", [P, TT, 2, TOK])
        dftg = sb("dftg", [P, 2, P])
        rope = sb("rope", [P, 2, TOK])
        rot = sb("rot", [P, P])
        masks = sb("masks", [P, TT, 2, TOK])
        iota = sb("iota", [P, TOPK])
        iota_b = sb("iota_b", [P, TOPK], BF16)
        ones = sb("ones", [P, P])
        onesb = sb("onesb", [P, P], BF16)
        eps = sb("eps", [P, 1])
        cols = sb("cols", [P, 5, P])
        silu_c = sb("silu_c", [P, KD, 2])
        mod = sb("mod", [P, DEPTH, 2, 48])
        lnrow = sb("lnrow", [P, 2, D])
        brow = sb("brow", [P, 5 * P])
        sink = sb("sink", [P, GQA_H])
        sg = sb("sg", [P, 2, TOK])
        bias = sb("bias", [P, TT, NAT_H, TOK])
        hpad = sb("hpad", [P, 2, TOK + TAPS - 1])
        nkb_c = sb("nkb_c", [P, 2, TOK])
        gkc = sb("gkc", [P, TOK])
        nvf_c = sb("nvf_c", [P, TT, 4 * P])
        gvb_c = sb("gvb_c", [P, TT, P])
        st8 = sb("st8", [P, 2, 8])
        bst = sb("bst", [P, 2, 6])
        mv = sb("mv", [P, 2])
        sd = sb("sd", [P, 2])
        gT = sb("gT", [P, TOK])
        eT = sb("eT", [P, TOK], U32)
        zcol = sb("zcol", [P, 2, GRP, 32])
        hcol = sb("hcol", [P, 2, GRP])
        ge = sb("ge", [P, 2, GRP])
        hsum = sb("hsum", [P, 2, HEADS])
        eidx = sb("eidx", [P, 2, 2, GRP], U32)
        cv, at = part(0, [4, TOK])
        hsq, hs_ = part(0, [2, TOK])
        hstd, hs_ = part(hs_, [TOK])
        hacc, at = part(at, [2, TOK])
        nq, at = part(at, [2, TOK])
        gqk, at = part(at, [5, TOK])
        nkb_l, at = part(at, [2, TOK])
        nvf_l, at = part(at, [TT, 4 * P])
        gvb_l, at = part(at, [TT, P])
        prod, at = part(at, [2, TOK])
        yb, at = part(at, [10, TOK])
        assert at <= RING * D
        fs, at = part(RING * D, [2, 2, TOK])
        Sm, at = part(at, [2, 2 * TOK])
        Pn, at = part(at, [2, 2 * TOK])
        PT, at = part(at, [2, 2 * TOK])
        uh, at = part(RING * D, [KD, TOK], F32R, of=split)
        ul, at = part(at, [KD, TOK], F32R, of=split)
        wh, at = part(at, [2, KD * P], F32R, of=split)
        wl, at = part(at, [2, KD * P], F32R, of=split)
        assert at <= 2 * RING * D

        def gate_w(slot, b):
            return W[:, slot, 0:4 * KD * P].rearrange("p (k b n) -> p k b n", k=KD, b=NB)[:, :, b, :]

        def high(b):
            return wh[:, b % 2, :].rearrange("p (k n) -> p k n", k=KD)

        def low(b):
            return wl[:, b % 2, :].rearrange("p (k n) -> p k n", k=KD)

        ada_out = nvf_c[0:2, :, :]
        ada_rows = nkb_c[0:96, 0, 0:P]
        nkb, nvf, gvb = [nkb_l, nkb_c], [nvf_l, nvf_c], [gvb_l, gvb_c]
        assert at <= 8 * 2048
        qT, at = part(0, [SEG, TOK])
        segs = [part(at + q * SEG * NKEY, [SEG, NKEY])[0] for q in range(TT)]
        kT, at = part(at + TT * SEG * NKEY, [SEG, NKEY])
        rest = [part(at + q * SEG * NKEY, [SEG, NKEY])[0] for q in range(TT)]
        cand, at = part(0, [HEADS, PAIRS], of=oT[:, :, :].rearrange("p k t -> p (k t)"))
        dec, _ = part(at, [6, HEADS * TOPK], of=oT[:, :, :].rearrange("p k t -> p (k t)"))
        cand_rest, _ = part(0, [HEADS, PAIRS], of=scratch[:, :, :].rearrange("p t d -> p (t d)"))
        hot, _ = part(KD * TOK, [HEADS * TOPK * TOPK // 2], BF16, of=um)
        hot = hot.rearrange("p (h k a) -> p h k a", h=HEADS, k=TOPK)
        spare_w = [W[:, q, 4 * KD * P:] for q in range(2)]
        v16, at = part(0, [TT * SEG, TOPK], of=spare_w[0])
        i16, at = part(at, [TT * SEG, TOPK], U32, of=spare_w[0])
        ts, at = part(at, [HEADS, TOPK], of=spare_w[0])
        pos, at = part(at, [HEADS, TOPK], U32, of=spare_w[0])
        assert at <= (WBLK - 4 * KD) * P
        i16f, at = part(0, [TT * SEG * TOPK // 2], BF16, of=spare_w[1])
        i16f = i16f.rearrange("p (g k) -> p g k", k=TOPK)
        ab, at = part(at, [2, HEADS * TOPK], U32, of=spare_w[1])
        abf, at = part(at, [HEADS * TOPK], BF16, of=spare_w[1])
        abf = abf.rearrange("p (e m) -> p e m", e=2)
        isel, at = part(at, [2, HEADS * TOPK], of=spare_w[1])
        assert at <= (WBLK - 4 * KD) * P
        Ur, at = part(0, [RING, D])
        Vr, at = part(at, [RING, D])
        uT, at = part(0, [KD, TOK], of=um)
        mT, _ = part(at, [KD, TOK], of=um)
        xs = um[:, at:at + 3 * D // 2].bitcast(BF16).rearrange("p (a b) -> p a b", a=3)
        xr = um[0:3, :].bitcast(BF16).rearrange("p (a b) -> p a b", a=2)
        ystage = oT[0:GRP, :, :].rearrange("p k t -> p (k t)").rearrange("p (h d) -> p h d", h=2)
        yrows, _ = part(KD * TOK, [TT, D], of=um)
        rows, _ = part(0, [5, P], of=oT[:, :, :].rearrange("p k t -> p (k t)"))
        ones3 = onesb[0:3, :]
        PS = es.enter_context(nc.psum_tensor("PS", [P, 8 * 512], F32))
        junk = scratch[:, 0, :]
        xrows = nc.dram_tensor("xrows", [3, TOK, 3, D], BF16, kind="Internal").ap()
        ada_d = nc.dram_tensor("ada_d", [DEPTH, 2, 6 * D], F32, kind="Internal").ap()
        ysum = nc.dram_tensor("ysum", [3, TOK, D], F32, kind="Internal").ap()
        spread_b = nc.dram_tensor("spread_b", [DEPTH, NAT_H, BANDS, GRID_W, PADW], F32, kind="Internal")
        ZROWS = DEPTH * NAT_H * BANDS * 2
        ZCOLS = GRID_W * PADW // 2

        def bank(i, a=0, b=512):
            return PS[:, i * 512 + a:i * 512 + b]

        first = sem("conditions_landed")
        consts = sem("consts_landed")
        set_up = sem("memsets_done")
        rows_t = sem("rows_transposed")
        cols_s = sem("columns_ready")
        silu_s = sem("silu_ready")
        padz = sem("rpb_zeroed")
        padr = sem("rpb_padded")
        w_land = [sem("weights_landed0"), sem("weights_landed1")]
        w_used = sem("weights_used")
        ada_p = sem("ada_product")
        ada_c = sem("ada_copied")
        ada_w = [sem("ada_written0"), sem("ada_written1")]
        ada_in = sem("ada_rows_landed")
        mod_p = sem("mod_product")
        mod_s = sem("mod_ready")
        lrow_s = sem("layer_rows_landed")
        ln_land = sem("norm_rows_landed")
        bias_s = sem("bias_landed")
        biasm_s = sem("bias_masked")
        dch_s = sem("vector_chain")
        pch_s = sem("gpsimd_chain")
        FP = [0, 1, 3]
        per_pass = dict(
            stat=2 * TT, std=2 * TT, xn=2 * TT, xnT=2 * TT, u_ready=2 * TT,
            unit=23, unit_act=19, unit_dve=4,
            ropemm=1, roped=1, S=24, sm=24, exp=24, pn=24, ptp=24, pts=24, O=24, y=24,
            conv_done=1, cmean=1, csq=1, cvar=1, cstd=1, cnorm=1, ya=1,
            xh=1, xl=1, wh=32, wl=32, gate=32, sig=32, merged=34, macc=8, wo=24, wo_s=24,
            resT=TT + 1, rstat=2 * TT, rstd=2 * TT, x_new=2 * TT,
            urow=TT, xsplit=TT, xs_dram=16 * TT, keysT=1, keys_s=4, sc_ps=8, sc_s=8,
            tsub=TT, texp=TT, sel=TT, selT=TT, sel_s=2 * TT, top=1, g2=1)
        keys_only = dict(stat=TT, std=TT, xn=TT, xnT=TT, u_ready=TT, unit=7, unit_act=3, unit_dve=4)
        stage = {n: sem(n) for n in per_pass}

        class Pass:

            def __init__(self, p):
                self.base = {}
                for n, c_ in per_pass.items():
                    made = [keys_only.get(n, 0) if PASSES[q][3] else
                            0 if n in ("ropemm", "roped") and PASSES[q][2] else c_ for q in range(p)]
                    self.base[n] = sum(made)

            def __getitem__(self, n):
                return stage[n]

            def at(self, n, v):
                return v + self.base[n]

        R = [Pass(p) for p in range(len(PASSES))]
        u_land = [sem(f"u_rows_landed{k}") for k in range(RING)]
        v_land = [sem(f"v_rows_landed{k}") for k in range(RING)]
        u_free = sem("u_slots_freed")
        v_free = sem("v_slots_freed")
        u_staged = sem("u_row_numbers_staged")
        v_staged = sem("v_row_numbers_staged")
        asked = sem("rows_asked")
        xr_land = [sem("x_rows_landed0"), sem("x_rows_landed1")]
        xr_free = sem("x_rows_freed")
        xb_s = sem("x_broadcast")
        gelu_s = sem("gelu_done")
        w_s = sem("expert_weights_ready")
        y_out = [sem("sums_written0"), sem("sums_written1")]
        y_in = sem("sums_landed")
        yc_s = sem("expert_sums_copied")
        out_s = sem("out_written")
        block = es.enter_context(nc.Block())

        NG = TOK // GRP // 2

        def full_index(p):
            return FP.index(p)

        @block.sync
        def _(sp):
            wt = Weights()

            def wtile(dsts, turn=None, first=None):
                n = wt.n
                slot, _ = wt.next(len(dsts))
                sp.wait_ge(w_used, n + 1 if turn is None else turn * 2 + (n + 1))
                for dst, src in dsts:
                    sp.dma_start(dst(slot), src).then_inc(w_land[slot], 16)

            def slot_view(blocks, width, at=0):
                return lambda s: W[:, s, at * P:at * P + blocks * width].rearrange("p (k n) -> p k n", k=blocks)

            xv = x[0].rearrange("(t p) d -> p t d", p=P)
            cxv = ctx[0].rearrange("(t p) d -> p t d", p=P)
            for dst, src in [(ident[:, :], ident_c),
                             (rows[0:8, 4, :], c.rearrange("a (k p) -> (a k) p", p=P)),
                             (rows[8:16, 4, :], c_ctx.rearrange("(k p) -> k p", p=P))]:
                sp.dma_start(dst, src).then_inc(first, 16)
            v = w_ada[0].rearrange("(k p) n -> p k n", p=P)
            for h in range(2):
                wtile([(slot_view(KD, 512), v[:, :, h * 512:(h + 1) * 512])])
            for dst, src in [(X[:, 1], cxv), (X[:, 0], xv), (dft[:, :, :, :], dft_c),
                             (dftg[:, :, :], dftg_c), (rope[:, :, :], rope_c), (rot[:, :], rot_c),
                             (masks[:, :, :, :], mask_c),
                             (iota[:, :], iota_c)]:
                sp.dma_start(dst, src).then_inc(consts, 16)
            for l in range(DEPTH):
                a = 2 * l
                for dst, src in [(rows[0:50, a, :], b_in[l].rearrange("(k p) -> k p", p=P)),
                                 (rows[R_ADA:R_CB, a, :], b_ada[l].rearrange("(k p) -> k p", p=P)),
                                 (rows[R_CB:R_CG, a, :], conv_b[l].rearrange("(k p) -> k p", p=P)),
                                 (rows[R_CG:R_CLB, a, :], conv_ln_g[l].rearrange("(k p) -> k p", p=P)),
                                 (rows[R_CLB:R_GQ, a, :], conv_ln_b[l].rearrange("(k p) -> k p", p=P)),
                                 (rows[R_GQ:R_END, a, :].rearrange("p (g d) -> p g d", g=2),
                                  b_in[l, C_GQ * P:C_GK * P].rearrange("(g h d) -> h g d", g=2, h=4)),
                                 (rows[0:2 * TAPS, a + 1, :], conv_w[l].rearrange("t (k p) -> (t k) p", p=P))]:
                    sp.dma_start(dst, src).then_inc(consts, 16)
            def spread_biases():
                sp.wait_ge(set_up, 1)
                sp.dma_start(spread_b.ap().rearrange("l h b (e c) w -> (l h b e) (c w)", e=2),
                             um[0:ZROWS, 0:ZCOLS]).then_inc(padz, 16)
                sp.wait_ge(padz, 16)
                lo = NAT_DR // 2 - (ROWS - 1)
                for l in range(DEPTH):
                    for h in range(NAT_H):
                        src = nat_rpb[l, h, lo:lo + BANDS, :].unsqueeze(1).to_broadcast([BANDS, GRID_W, RPB_W])
                        dst = bass.AP(spread_b, (l * NAT_H + h) * BANDS * GRID_W * PADW,
                                      [[GRID_W * PADW, BANDS], [PADW + 1, GRID_W], [1, RPB_W]])
                        sp.dma_start(dst, src).then_inc(padr, 16)
                sp.wait_ge(padr, 16 * DEPTH * NAT_H)

            def layer_rows(l):
                sp.dma_start(brow[:, 0:4 * P], b_in[l, C_NV * P:C_GQ * P].partition_broadcast(P)).then_inc(lrow_s, 16)
                sp.dma_start(brow[:, 4 * P:5 * P],
                             b_in[l, C_GV * P:C_GATE * P].partition_broadcast(P)).then_inc(lrow_s, 16)
                sp.dma_start(sink[:, :], gqa_sink[l].partition_broadcast(P)).then_inc(lrow_s, 16)
                for r in range(ROWS):
                    for h in range(NAT_H):
                        src = bass.AP(spread_b, ((l * NAT_H + h) * BANDS + ROWS - 1 - r) * GRID_W * PADW + RPB_W // 2,
                                      [[PADW, GRID_W], [GRID_W * PADW, ROWS], [1, GRID_W]])
                        dst = bias[(r % 2) * GRID_W:(r % 2 + 1) * GRID_W, r // 2, h, :]
                        sp.dma_start(dst.rearrange("p (w c) -> p w c", w=ROWS), src).then_inc(bias_s, 16)

            def ada(l):
                v = w_ada[l].rearrange("(k p) n -> p k n", p=P)
                done = 0 if l else 1
                with sp.Fori(0, 6 - done) as i:
                    for h in range(2):
                        wtile([(slot_view(KD, 512), v[:, :, bass.ds(i * 1024 + (done * 1024 + h * 512), 512)])], i)
                wt.skip(10 - 2 * done, 1)

            def ada_back(l):
                for h in range(2):
                    sp.wait_ge(ada_w[h], 16 + 16 * 6 * (l + 1))
                sp.dma_start(ada_rows, ada_d[l].rearrange("s (n p) -> (s n) p", p=P)).then_inc(ada_in, 16)

            lns = [0]

            def ln_rows(g, b, q, tiles):
                if lns[0]:
                    sp.wait_ge(R[q]["x_new"], R[q].at("x_new", tiles))
                lns[0] += 1
                sp.dma_start(lnrow[:, 0, :], g.partition_broadcast(P)).then_inc(ln_land, 16)
                sp.dma_start(lnrow[:, 1, :], b.partition_broadcast(P)).then_inc(ln_land, 16)

            for p, (name, l, s, kv) in enumerate(PASSES):
                wi = w_in[l].rearrange("(k p) n -> p k n", p=P)
                if p == 0:
                    ada(0)
                    spread_biases()
                    wtile([(slot_view(KD, 512), wi[:, :, 0:512])])
                    ada_back(0)
                    wtile([(slot_view(KD, 512), wi[:, :, 512:1024])])
                    layer_rows(0)
                if kv:
                    for t in (1, 2):
                        wtile([(slot_view(KD, 512), wi[:, :, t * 512:(t + 1) * 512])])
                else:
                    for t in range(0 if p else 2, 3):
                        wtile([(slot_view(KD, 512), wi[:, :, t * 512:(t + 1) * 512])])
                    wtile([(lambda s_, g=g, j=j: W[:, s_, 0:KD * 512].rearrange(
                        "p (k h g d) -> p k h g d", k=KD, h=4, g=2)[:, :, j, g, :],
                        wi[:, :, C_GQ * P + (g * 4 + j) * DH:C_GQ * P + (g * 4 + j + 1) * DH])
                        for g in range(2) for j in range(4)])
                wtile([(slot_view(KD, 256), wi[:, :, 2048:2304])])
                if kv:
                    continue
                gv = wi[:, :, C_GATE * P:].rearrange("p k (b n) -> p k b n", b=NB)
                br = [w[l].rearrange("(k p) n -> p k n", p=P) for w in (w_branch_a, w_branch_b, w_branch_c, w_branch_d)]
                with sp.Fori(0, 4) as i:
                    for h in range(2):
                        j = bass.ds(i * (2 * P) + h * P, P)
                        dsts, at = [], 32
                        for b in range(NB):
                            dsts.append((lambda s, b=b: W[:, s, 0:32 * P].rearrange(
                                "p (k b n) -> p k b n", k=KD, b=NB)[:, :, b, :], gv[:, :, b, j]))
                        for w, kt in zip(br, (2, 2, 2, 4)):
                            dsts.append((slot_view(kt, P, at), w[:, :, j]))
                            at += kt
                        wtile(dsts, i)
                wt.skip(6, 8)
                wo = w_out[l].rearrange("(k p) n -> p k n", p=P)
                for t in range(2):
                    wtile([(slot_view(KD, 512), wo[:, :, t * 512:(t + 1) * 512])])
                ln_rows(ln1_g[l], ln1_b[l], FP[full_index(p) - 1], 2 * TT)
                wq = peer_wq[l].rearrange("(k p) n -> p k n", p=P)
                wtile([(slot_view(HEADS, P), peer_k1[l].rearrange("h n k -> n h k")),
                       (slot_view(HEADS, P, HEADS), peer_k2[l].rearrange("h n k -> n h k"))])
                for t in range(4):
                    wtile([(slot_view(KD, 512), wq[:, :, t * 512:(t + 1) * 512])])
                ln_rows(ln2_g[l], ln2_b[l], p, TT)
                if p == 1:
                    sp.wait_ge(R[p]["y"], R[p].at("y", 24))
                    layer_rows(1)
                    ada(1)
                    ada_back(1)
                f = full_index(p)
                sp.wait_ge(R[p]["xs_dram"], R[p].at("xs_dram", 16 * TT))
                sp.wait_ge(R[p]["wo_s"], R[p].at("wo_s", 24))
                sp.wait_ge(R[p]["sel"], R[p].at("sel", TT))
                xv3 = xrows[f].rearrange("t q d -> q t d")
                with sp.Fori(0, NG) as i:
                    for h in range(2):
                        sp.wait_ge(xr_free, i * 2 + (f * 2 * NG + h + 1))
                        sp.dma_start(xr[:, h, :].rearrange("q (t d) -> q t d", t=GRP),
                                     xv3[:, bass.ds(i * (2 * GRP) + h * GRP, GRP), :]).then_inc(xr_land[h], 16)
                for h in range(2):
                    sp.wait_ge(y_out[h], 16 + 16 * NG * (f + 1))
                sp.dma_start(yrows[:, :, :], ysum[f].rearrange("(t p) d -> p t d", p=P)).then_inc(y_in, 16)
            sp.wait_ge(R[3]["x_new"], R[3].at("x_new", 2 * TT))
            sp.dma_start(out[0].rearrange("(t p) d -> p t d", p=P), X[:, 0]).then_inc(out_s, 16)
            sp.wait_ge(out_s, 16)

        @block.gpsimd
        def _(pool):
            nc.gpsimd.memset(um[:, :], 0.0).then_inc(set_up, 1)
            nc.gpsimd.memset(ones[:, :], 1.0 / 256.0).then_inc(set_up, 1)
            nc.gpsimd.memset(onesb[:, :], 1.0).then_inc(set_up, 1)
            nc.gpsimd.memset(eps[:, :], LN_EPS).then_inc(set_up, 1)
            nc.gpsimd.memset(hpad[:, :, :], 0.0).then_inc(set_up, 1)
            nc.gpsimd.memset(zcol[:, :, :, :], 0.0).then_inc(set_up, 1)
            pool.wait_ge(set_up, 6)
            ch = Chain(pool, pch_s)
            for p in FP:
                f = full_index(p)
                l = PASSES[p][1]
                ut = (peer_u0, peer_u1)[l]
                vt = (peer_v0, peer_v1)[l]
                a = 2 * l
                G = nc.gpsimd
                r = R[p]
                pool.wait_ge(r["unit_act"], r.at("unit_act", 4))
                half = TAPS // 2
                ch.link(G.tensor_tensor(hpad[:, :, half:half + TOK], cv[:, 0:2, :], cv[:, 2:4, :], ALU.mult))
                for t in range(TAPS):
                    both = [P, 2, TOK]
                    tap = cols[:, a + 1, 2 * t:2 * t + 2].unsqueeze(2).to_broadcast(both)
                    part_ = (sg, prod)[t % 2]
                    ch.link(G.tensor_tensor(part_[:, :, :], hpad[:, :, t:t + TOK], tap, ALU.mult))
                    acc = hacc[:, :, :] if t else cols[:, a, R_CB:R_CB + 2].unsqueeze(2).to_broadcast(both)
                    ins = G.tensor_tensor(hacc[:, :, :], acc, part_[:, :, :], ALU.add)
                    if t == TAPS - 1:
                        ins.then_inc(r["conv_done"], 1)
                    else:
                        ch.add(ins)
                for tt in range(TT):
                    pool.wait_ge(R[p]["xsplit"], R[p].at("xsplit", tt + 1))
                    pool.dma_start(xrows[f, tt * P:(tt + 1) * P], xs[:, :, :]).then_inc(R[p]["xs_dram"], 16)
                pool.wait_ge(R[p]["sel_s"], R[p].at("sel_s", 2))
                pool.wait_ge(R[p]["sc_s"], R[p].at("sc_s", 4 * TT))
                pool.wait_ge(R[p]["top"], R[p].at("top", 1))

                def gather_u(i, h):
                    pool.wait_ge(u_free, i * (2 * GRP) + (f * TOK + (h + 1) * GRP))
                    pool.sem_inc(asked, 1)
                    nc.gpsimd.tensor_copy(eidx[:, 0, h, :], eT[:, bass.ds(i * (2 * GRP) + h * GRP, GRP)])\
                        .then_inc(u_staged, 1)
                    pool.wait_ge(u_staged, i * 2 + (f * 2 * NG + h + 1))
                    pool.sem_inc(asked, 1)
                    for k in range(GRP):
                        pool.indirect_dma_start(Ur[:, h * GRP + k, :], None, ut,
                                                bass.IndirectOffsetOnAxis(eidx[:, 0, h, k:k + 1], 0))\
                            .then_inc(u_land[h * GRP + k], 16)

                def gather_v(i, h):
                    pool.wait_ge(v_free, i * 2 + (f * 2 * NG + h + 1))
                    pool.sem_inc(asked, 1)
                    nc.gpsimd.tensor_copy(eidx[:, 1, h, :], eT[:, bass.ds(i * (2 * GRP) + h * GRP, GRP)])\
                        .then_inc(v_staged, 1)
                    pool.wait_ge(v_staged, i * 2 + (f * 2 * NG + h + 1))
                    pool.sem_inc(asked, 1)
                    for k in range(GRP):
                        pool.indirect_dma_start(Vr[:, h * GRP + k, :], None, vt,
                                                bass.IndirectOffsetOnAxis(eidx[:, 1, h, k:k + 1], 0))\
                            .then_inc(v_land[h * GRP + k], 16)

                for h in range(2):
                    gather_u(0, h)
                with pool.Fori(0, NG - 1) as i:
                    for h in range(2):
                        gather_v(i, h)
                        gather_u(i + 1, h)
                for h in range(2):
                    gather_v(NG - 1, h)

        @block.tensor
        def _(pe):
            wt = Weights()
            T = nc.tensor

            def arrived(dmas, turn=None, per=None):
                slot, v = wt.next(dmas)
                pe.wait_ge(w_land[slot], v if turn is None else turn * (16 * dmas) + v)
                return slot

            pe.sem_inc(w_used, 2)
            pe.sem_inc(v_free, 2)
            pe.sem_inc(xr_free, 2)
            pe.wait_ge(first, 16 * 3)
            T.transpose(bank(4, 0, 16), rows[0:16, 4, :], ident[0:16, 0:16]).then_inc(rows_t, 1)
            pe.wait_ge(set_up, 6)

            def echo(s):
                T.matmul(bank(7, 508, 510), onesb[:, :], onesb[:, 0:2], start=True, stop=True).then_inc(s, 1)

            def ada(l, first, turns):
                with pe.Fori(0, turns) as i:
                    for h in range(2):
                        s = arrived(1, i)
                        pe.wait_ge(ada_c, i * 2 + (12 * l + 2 * first + h + 1))
                        for k in range(KD):
                            last = T.matmul(PS[0:2, (2 * h) * 512:(2 * h + 1) * 512], silu_c[:, k, :],
                                            W[:, s, k * 512:(k + 1) * 512], start=(k == 0), stop=(k == KD - 1))
                        last.then_inc(ada_p, 1)
                        echo(w_used)
                wt.skip(2 * turns - 2, 1)

            def ada_columns(l):
                pe.wait_ge(ada_in, 16 * (l + 1))
                T.transpose(bank(7, 0, 96), ada_rows, ident[0:96, 0:96]).then_inc(mod_p, 1)

            def transposes(p, src, a, ready, count, done):
                for tt in range(TT):
                    pe.wait_ge(R[p][ready], R[p].at(ready, count + tt + 1))
                    for k in range(KD):
                        last = T.transpose(bank(2 * tt + k // 4, (k % 4) * P, (k % 4 + 1) * P),
                                           src[:, tt, k * P:(k + 1) * P], ident[:, :])
                    last.then_inc(R[p][done], 1)

            def back(p, src, b, done):
                for tt in range(TT):
                    for k in range(KD):
                        last = T.transpose(bank(b + 2 * tt + k // 4, (k % 4) * P, (k % 4 + 1) * P),
                                           src[:, k, tt * P:(tt + 1) * P], ident[:, :])
                    last.then_inc(R[p][done], 1)

            for p, (name, l, s, kv) in enumerate(PASSES):
                r = R[p]
                if p == 0:
                    pe.wait_ge(silu_s, 1)
                    ada(0, 0, 6)
                    pe.wait_ge(consts, 16 * 22)
                    for q, n in enumerate([R_END, 2 * TAPS, R_END, 2 * TAPS]):
                        last = T.transpose(bank((1, 3, 5, 6)[q], 0, n), rows[0:n, q, :], ident[0:n, 0:n])
                    last.then_inc(rows_t, 1)
                    ada_columns(0)
                    pe.wait_ge(cols_s, 2)
                    pe.wait_ge(ada_c, 12 + 2)
                transposes(p, scratch, 0, "xn", 0, "xnT")
                pe.wait_ge(r["u_ready"], r.at("u_ready", TT))
                units = units_of(s, kv)
                kinds = [u[0] in "TQ" for u in units]
                slot = None
                for n, (kind, tile, blk, dst) in enumerate(units):
                    if not n or units[n - 1][1] != tile:
                        slot = arrived(8 if kind == "Q" else 1)
                    if n >= 4:
                        m = n - 4
                        if kinds[m]:
                            pe.wait_ge(r["unit_act"], r.at("unit_act", sum(kinds[:m + 1])))
                        else:
                            pe.wait_ge(r["unit_dve"], r.at("unit_dve", m + 1 - sum(kinds[:m + 1])))
                    width = 256 if tile == 4 else 512
                    for k in range(KD):
                        wk = W[:, slot, k * width:(k + 1) * width]
                        go = dict(start=(k == 0), stop=(k == KD - 1))
                        if kind in "TQ":
                            last = T.matmul(bank(n % 4, 0, TOK), wk[:, blk * P:(blk + 1) * P], uT[:, k, :], **go)
                        elif kind == "N":
                            last = T.matmul(bank(n % 4), uT[:, k, dst * P:(dst + 1) * P], wk, **go)
                        else:
                            last = T.matmul(bank(n % 4, 0, P), uT[:, k, dst * P:(dst + 1) * P], wk[:, P:2 * P], **go)
                    last.then_inc(r["unit"], 1)
                    if n + 1 == len(units) or units[n + 1][1] != tile:
                        echo(w_used)
                if kv:
                    continue
                na = sum(kinds)
                nv = len(units) - na
                pe.wait_ge(r["unit_dve"], r.at("unit_dve", nv))
                pe.wait_ge(r["unit_act"], r.at("unit_act", na))
                for q in range(4):
                    cs, ct = q // 2, q % 2
                    for tt in range(TT):
                        last = T.matmul(bank(q, 0, TOK), nvf[s][:, tt, 2 * P + ct * P:2 * P + (ct + 1) * P],
                                        dft[:, tt, cs, :], start=(tt == 0), stop=(tt == TT - 1))
                    last.then_inc(r["unit"], 1)
                pe.wait_ge(r["unit_act"], r.at("unit_act", na + 4))
                for ct in range(2):
                    for cs in range(2):
                        last = T.matmul(bank(ct, 0, TOK), dftg[:, cs, :], fs[:, cs, ct, :],
                                        start=(cs == 0), stop=(cs == 1))
                    last.then_inc(r["unit"], 1)
                if s == 0:
                    for q in range(5):
                        last = T.matmul(PS[:, 4 * 512 + q * TOK:4 * 512 + (q + 1) * TOK], rot[:, :], gqk[:, q, :],
                                        start=True, stop=True)
                    last.then_inc(r["ropemm"], 1)
                    pe.wait_ge(r["roped"], r.at("roped", 1))
                jobs = attention_jobs()
                pe.wait_ge(r["unit_act"], r.at("unit_act", na + 6))

                def scores(n):
                    br, h, qt = jobs[n]
                    if n >= 3:
                        pe.wait_ge(r["sm"], r.at("sm", n - 2))
                    if br == 0:
                        o = (h % 2) * DH
                        q_ = nq[o:o + DH, h // 2, qt * P:(qt + 1) * P]
                        ks = [nkb[st][o:o + DH, h // 2, :] for st in ((0, 1) if s == 0 else (1,))]
                    else:
                        o = (h // 4) * DH
                        q_ = gqk[o:o + DH, h % 4, qt * P:(qt + 1) * P]
                        ks = [gqk[o:o + DH, 4, :], gkc[o:o + DH, :]] if s == 0 else [gkc[o:o + DH, :]]
                    for m, k_ in enumerate(ks):
                        last = T.matmul(bank(SBANK[n % 3], m * TOK, (m + 1) * TOK), q_, k_, start=True, stop=True)
                    last.then_inc(r["S"], 1)

                nk = 4 if s == 0 else 2

                def transposed(n):
                    pe.wait_ge(r["pn"], r.at("pn", n + 1))
                    if n >= 2:
                        pe.wait_ge(r["pts"], r.at("pts", n - 1))
                    for q in range(nk):
                        last = T.transpose(bank(2 + n % 2, q * P, (q + 1) * P), Pn[:, n % 2, q * P:(q + 1) * P],
                                           ident[:, :])
                    last.then_inc(r["ptp"], 1)

                def values(n):
                    br, h, qt = jobs[n]
                    pe.wait_ge(r["pts"], r.at("pts", n + 1))
                    if n >= 2:
                        pe.wait_ge(r["y"], r.at("y", n - 1))
                    o = (h % 2) * DH
                    for q in range(nk):
                        st = (0, 0, 1, 1)[q] if s == 0 else 1
                        if br == 0:
                            v_ = nvf[st][:, q % 2, h * DH:(h + 1) * DH]
                        else:
                            v_ = gvb[st][:, q % 2, (h // 4) * DH:(h // 4 + 1) * DH]
                        last = T.matmul(PS[o:o + DH, (4 + n % 2) * 512:(4 + n % 2) * 512 + P], v_,
                                        PT[:, n % 2, q * P:(q + 1) * P], start=(q == 0), stop=(q == nk - 1))
                    last.then_inc(r["O"], 1)

                scores(0)
                for n in range(len(jobs) + 2):
                    if n + 1 < len(jobs):
                        scores(n + 1)
                    if 1 <= n <= len(jobs):
                        transposed(n - 1)
                    if n >= 2:
                        values(n - 2)
                pe.wait_ge(r["conv_done"], r.at("conv_done", 1))
                for q in range(2):
                    last = T.matmul(bank(6, 0, TOK), ones[:, :], hacc[:, q, :], start=(q == 0), stop=(q == 1))
                last.then_inc(r["cmean"], 1)
                pe.wait_ge(r["csq"], r.at("csq", 1))
                for q in range(2):
                    last = T.matmul(bank(6, TOK, 2 * TOK), ones[:, :], hsq[:, q, :], start=(q == 0), stop=(q == 1))
                last.then_inc(r["cvar"], 1)
                pe.wait_ge(r["y"], r.at("y", len(jobs)))
                pe.wait_ge(r["ya"], r.at("ya", 1))
                pe.wait_ge(r["xl"], r.at("xl", 1))
                with pe.Fori(0, 4) as i:
                    for h in range(2):
                        s_ = arrived(8, i)
                        at = 32
                        for b, kt in enumerate((2, 2, 2, 4)):
                            pe.wait_ge(r["merged"], r.at("merged", i * 8 + (h * 4 + b + 1)))
                            pe.wait_ge(r["wl"], r.at("wl", i * 8 + (h * 4 + b + 1)))
                            terms = [(w_[:, k, :], u_[:, k, :]) for k in range(KD)
                                     for w_, u_ in ((high(b), uh), (high(b), ul), (low(b), uh))]
                            for n, (w_, u_) in enumerate(terms):
                                T.matmul(bank(b % 2, 0, TOK), w_, u_, start=(n == 0), stop=(n == len(terms) - 1))
                            for k in range(kt):
                                last = T.matmul(bank(b % 2, TOK, 2 * TOK), W[:, s_, (at + k) * P:(at + k + 1) * P],
                                                yb[:, at - 32 + k, :], start=(k == 0), stop=(k == kt - 1))
                            at += kt
                            last.then_inc(r["gate"], 1)
                        echo(w_used)
                wt.skip(6, 8)
                pe.wait_ge(r["macc"], r.at("macc", 8))

                def outT(t, src, base):
                    s_ = arrived(1)
                    for j in range(4):
                        n = 4 * t + j
                        if n >= 4:
                            pe.wait_ge(r["wo_s"], r.at("wo_s", base + n - 3))
                        for k in range(KD):
                            last = T.matmul(bank(n % 4, 0, TOK), W[:, s_, k * 512 + j * P:k * 512 + (j + 1) * P],
                                            src[:, k, :], start=(k == 0), stop=(k == KD - 1))
                        last.then_inc(r["wo"], 1)
                        if base and t and j == 0:
                            pe.wait_ge(r["wo"], r.at("wo", base + 4 * t))
                            pe.sem_inc(w_used, 1)
                    if not base:
                        echo(w_used)

                for t in range(2):
                    outT(t, mT, 0)
                s_ = arrived(2)
                for q in range(SEG):
                    h, half = q // 2, q % 2
                    last = T.transpose(bank(4 + q // 4, (q % 4) * P, (q % 4 + 1) * P),
                                       W[:, s_, (half * HEADS + h) * P:(half * HEADS + h + 1) * P], ident[:, :])
                last.then_inc(r["keysT"], 1)
                pe.wait_ge(r["wo_s"], r.at("wo_s", 8))
                back(p, oT, 0, "resT")
                pe.wait_ge(r["keys_s"], r.at("keys_s", 4))
                echo(w_used)
                transposes(p, scratch, 0, "xn", TT, "xnT")
                pe.wait_ge(r["u_ready"], r.at("u_ready", 2 * TT))
                back(p, uT, 4, "urow")

                for t in range(5):
                    if t < 4:
                        outT(t, uT, 8)
                    if t:
                        pe.wait_ge(r["wo_s"], r.at("wo_s", 8 + 4 * t))
                        if t == 4:
                            pe.sem_inc(w_used, 1)
                        for tt in range(TT):
                            n = 2 * (t - 1) + tt
                            if t == 1:
                                pe.wait_ge(r["xsplit"], r.at("xsplit", TT))
                            elif t > 2:
                                pe.wait_ge(r["sc_s"], r.at("sc_s", n - 3))
                            for j in range(4):
                                q = 4 * (t - 1) + j
                                last = T.matmul(bank(4 + n % 4, j * P, (j + 1) * P), qT[:, q, tt * P:(tt + 1) * P],
                                                kT[:, q, :], start=True, stop=True)
                            last.then_inc(r["sc_ps"], 1)
                if p == 1:
                    pe.wait_ge(r["sc_s"], r.at("sc_s", 8))
                for tt in range(TT):
                    if p == 1:
                        ada(1, 2 * tt, (2, 4)[tt])
                    pe.wait_ge(r["sel"], r.at("sel", tt + 1))
                    T.transpose(bank(4 + tt, 0, P), isel[:, 0, :], ident[:, :])
                    T.transpose(bank(4 + tt, P, 2 * P), ts[:, :, :].rearrange("p h k -> p (h k)"), ident[:, :])\
                        .then_inc(r["selT"], 1)
                pe.wait_ge(r["sel_s"], r.at("sel_s", 2 * TT))
                if p == 1:
                    ada_columns(1)
                    pe.wait_ge(mod_s, DEPTH)
                f = full_index(p)

                def broadcast(i, h, k):
                    if k == 0:
                        pe.wait_ge(xr_land[h], i * 16 + (f * NG * 16 + 16))
                    pe.wait_ge(u_free, i * (2 * GRP) + (f * TOK + h * GRP + k + RING - 1))
                    for q in range(2):
                        last = T.matmul(bank(2 * (k % 2) + q), ones3,
                                        xr[:, h, k * D + q * 512:k * D + (q + 1) * 512], start=True, stop=True)
                    last.then_inc(xb_s, 1)
                    if k == GRP - 1:
                        T.matmul(PS[96:128, 7 * 512 + 508:7 * 512 + 510], onesb[:, 0:32], onesb[:, 0:2],
                                 start=True, stop=True).then_inc(xr_free, 1)

                def weigh(i, h, k):
                    if k == 0:
                        pe.wait_ge(w_s, i * 2 + (f * 2 * NG + h + 1))
                        pe.wait_ge(yc_s, i * 2 + (f * 2 * NG + h + 1))
                    pe.wait_ge(v_land[h * GRP + k], i * 16 + (f * NG * 16 + 16))
                    for q in range(2):
                        last = T.matmul(PS[0:32, (4 + 2 * h + q) * 512:(5 + 2 * h + q) * 512], zcol[:, h, k, :],
                                        Vr[:, h * GRP + k, q * 512:(q + 1) * 512],
                                        start=(k == 0), stop=(k == GRP - 1))
                    if k == GRP - 1:
                        last.then_inc(v_free, 1)

                for h in range(2):
                    for k in range(GRP):
                        broadcast(0, h, k)
                with pe.Fori(0, NG - 1) as i:
                    for h in range(2):
                        for k in range(GRP):
                            weigh(i, h, k)
                            broadcast(i + 1, h, k)
                for h in range(2):
                    for k in range(GRP):
                        weigh(NG - 1, h, k)
                pe.wait_ge(r["g2"], r.at("g2", 1))
                for k in range(KD):
                    last = T.matmul(bank(4 + k // 4, (k % 4) * P, (k % 4 + 1) * P), mod[:, l, s, 40 + k:41 + k].to_broadcast([P, P]),
                                    ident[:, :], start=True, stop=True)
                last.then_inc(r["resT"], 1)

        @block.scalar
        def _(act):
            A = nc.scalar.activation
            act.sem_inc(yc_s, 2)
            act.sem_inc(y_out[0], 16)
            act.sem_inc(y_out[1], 16)
            act.sem_inc(ada_c, 2)
            act.sem_inc(ada_w[0], 16)
            act.sem_inc(ada_w[1], 16)
            act.wait_ge(cols_s, 1)
            A(silu_c[:, :, :].rearrange("p k s -> p s k"), cols[:, 4, 0:16].rearrange("p (s k) -> p s k", s=2),
              ACT.Silu).then_inc(silu_s, 1)
            act.wait_ge(set_up, 6)

            def spread(p, stat, std, count):
                act.wait_ge(R[p][stat], R[p].at(stat, count))
                A(sd[:, 0:1], mv[:, 1:2], ACT.Sqrt, bias=eps[:, 0:1]).then_inc(R[p][std], 1)

            def modulate(p, l, s, base, shift, scale):
                r = R[p]
                if p or base:
                    for tt in range(TT):
                        spread(p, "stat", "std", base + tt + 1)
                act.wait_ge(mod_s, l + 1)
                for tt in range(TT):
                    act.wait_ge(r["xnT"], r.at("xnT", base + tt + 1))
                    for k in range(KD):
                        last = A(uT[:, k, tt * P:(tt + 1) * P], bank(2 * tt + k // 4, (k % 4) * P, (k % 4 + 1) * P),
                                 ACT.Identity, scale=mod[:, l, s, scale + k:scale + k + 1],
                                 bias=mod[:, l, s, shift + k:shift + k + 1])
                    last.then_inc(r["u_ready"], 1)

            def ada(l, first, turns):
                with act.Fori(0, turns) as i:
                    for h in range(2):
                        act.wait_ge(ada_p, i * 2 + (12 * l + 2 * first + h + 1))
                        act.wait_ge(ada_w[h], i * 16 + (16 * (6 * l + first) + 16))
                        A(ada_out[:, h, :], PS[0:2, (2 * h) * 512:(2 * h + 1) * 512], ACT.Copy).then_inc(ada_c, 1)
                        act.wait_ge(ada_c, i * 2 + (12 * l + 2 * first + h + 3))
                        act.dma_start(ada_d[l, :, bass.ds(i * 1024 + (first * 1024 + h * 512), 512)], ada_out[:, h, :])\
                            .then_inc(ada_w[h], 16)

            ada(0, 0, 1)
            for tt in range(TT):
                spread(0, "stat", "std", tt + 1)
            ada(0, 1, 5)
            for p, (name, l, s, kv) in enumerate(PASSES):
                r = R[p]
                a = 2 * l
                modulate(p, l, s, 0, 0, 8)
                if p and not PASSES[p - 1][3]:
                    for tt in range(TT):
                        spread(p - 1, "rstat", "rstd", TT + tt + 1)
                dst_of = {"cv": lambda j: cv[:, j, :], "nq": lambda j: nq[:, j, :], "nk": lambda j: nkb[s][:, j, :],
                          "gq": lambda j: gqk[:, j, :], "gk": lambda j: gqk[:, 4, :] if s == 0 else gkc[:, :]}
                units = units_of(s, kv)
                for n, (kind, tile, blk, dst) in enumerate(units):
                    if kind in "TQ":
                        col = R_GQ + blk if kind == "Q" else 4 * tile + blk
                        act.wait_ge(r["unit"], r.at("unit", n + 1))
                        fn = ACT.Sigmoid if dst[0] == "cv" and dst[1] >= 2 else ACT.Identity
                        A(dst_of[dst[0]](dst[1]), bank(n % 4, 0, TOK), fn, bias=cols[:, a, col:col + 1])\
                            .then_inc(r["unit_act"], 1)
                if kv:
                    continue
                nu = len(units)
                for q in range(4):
                    act.wait_ge(r["unit"], r.at("unit", nu + q + 1))
                    A(fs[:, q // 2, q % 2, :], bank(q, 0, TOK), ACT.Copy).then_inc(r["unit_act"], 1)
                for q in range(2):
                    act.wait_ge(r["unit"], r.at("unit", nu + 4 + q + 1))
                    A(yb[:, 4 + q, :], bank(q, 0, TOK), ACT.Copy).then_inc(r["unit_act"], 1)
                jobs = attention_jobs()
                w = 2 * TOK if s == 0 else TOK

                def exps(n):
                    br, h, qt = jobs[n]
                    q = n % 2
                    act.wait_ge(r["sm"], r.at("sm", n + 1))
                    if n >= 2:
                        act.wait_ge(r["ptp"], r.at("ptp", n - 1))
                    last = A(Pn[:, q, 0:w], Sm[:, q, 0:w], ACT.Exp, bias=st8[:, q, 1:2], accum_out=st8[:, q, 2:3])
                    if br:
                        last = A(st8[:, q, 3:4], sink[:, h:h + 1], ACT.Exp, bias=st8[:, q, 1:2])
                    last.then_inc(r["exp"], 1)

                def probs(n):
                    q = n % 2
                    act.wait_ge(r["ptp"], r.at("ptp", n + 1))
                    if n >= 2:
                        act.wait_ge(r["O"], r.at("O", n - 1))
                    A(PT[:, q, 0:w], bank(2 + q, 0, w), ACT.Copy).then_inc(r["pts"], 1)

                def outputs(n):
                    br, h, qt = jobs[n]
                    q = n % 2
                    act.wait_ge(r["O"], r.at("O", n + 1))
                    o = (h % 2) * DH
                    A(yb[o:o + DH, (2, 6)[br] + h // 2, qt * P:(qt + 1) * P],
                      PS[o:o + DH, (4 + q) * 512:(4 + q) * 512 + P], ACT.Copy).then_inc(r["y"], 1)

                for n in range(len(jobs) + 2):
                    if n < len(jobs):
                        exps(n)
                    if 1 <= n <= len(jobs):
                        probs(n - 1)
                    if n >= 2:
                        outputs(n - 2)
                A(uh[:, :, :], uT[:, :, :], ACT.Copy).then_inc(r["xh"], 1)
                tiles = merge_tiles(p)

                def split_high(i, h, b):
                    slot, landed = tiles[h]
                    act.wait_ge(w_land[slot], i * (16 * 8) + landed)
                    A(high(b), gate_w(slot, b), ACT.Copy).then_inc(r["wh"], 1)

                split_high(0, 0, 0)
                split_high(0, 0, 1)
                act.wait_ge(r["cvar"], r.at("cvar", 1))
                A(hstd[:, :], bank(6, TOK, 2 * TOK), ACT.Sqrt, bias=eps[:, 0:1]).then_inc(r["cstd"], 1)
                act.wait_ge(r["cnorm"], r.at("cnorm", 1))
                for q in range(2):
                    last = A(yb[:, q, :], hacc[:, q, :], ACT.Silu, scale=cols[:, a, R_CG + q:R_CG + q + 1],
                             bias=cols[:, a, R_CLB + q:R_CLB + q + 1])
                last.then_inc(r["ya"], 1)
                def gate(i, h, b, ahead):
                    act.wait_ge(r["gate"], r.at("gate", i * 8 + (h * 4 + b + 1)))
                    if ahead:
                        split_high(i + ahead[0], ahead[1], ahead[2])
                    A(sg[:, b % 2, :], bank(b % 2, 0, TOK), ACT.Sigmoid,
                      bias=cols[:, a, bass.ds(i * 2 + (C_GATE + b * KD + h), 1)]).then_inc(r["sig"], 1)

                with act.Fori(0, 3) as i:
                    for h, b, ahead in merge_steps():
                        gate(i, h, b, ahead)
                for h, b, ahead in merge_steps():
                    gate(3, h, b, None if ahead[0] else ahead)
                for n in range(KD):
                    act.wait_ge(r["wo"], r.at("wo", n + 1))
                    A(oT[:, n, :], bank(n % 4, 0, TOK), ACT.Copy, scale=mod[:, l, s, 16 + n:17 + n])\
                        .then_inc(r["wo_s"], 1)
                act.wait_ge(r["keysT"], r.at("keysT", 1))
                for q in range(4):
                    A(kT[:, 4 * q:4 * q + 4, :].rearrange("p a n -> p (a n)"), bank(4 + q), ACT.Copy)\
                        .then_inc(r["keys_s"], 1)
                for tt in range(TT):
                    spread(p, "rstat", "rstd", tt + 1)
                modulate(p, l, s, TT, 24, 32)
                for t in range(5):
                    if t < 4:
                        for n in range(4 * t, 4 * t + 4):
                            act.wait_ge(r["wo"], r.at("wo", 8 + n + 1))
                            A(qT[:, n, :], bank(n % 4, 0, TOK), ACT.Copy).then_inc(r["wo_s"], 1)
                    if t:
                        for tt in range(TT):
                            n = 2 * (t - 1) + tt
                            act.wait_ge(r["sc_ps"], r.at("sc_ps", n + 1))
                            A(segs[tt][:, 4 * t - 4:4 * t, :].rearrange("p a n -> p (a n)"), bank(4 + n % 4), ACT.Copy)\
                                .then_inc(r["sc_s"], 1)
                for tt in range(TT):
                    if p == 1:
                        ada(1, 2 * tt, (2, 4)[tt])
                    act.wait_ge(r["tsub"], r.at("tsub", tt + 1))
                    A(ts[:, :, :], ts[:, :, :], ACT.Exp).then_inc(r["texp"], 1)
                    act.wait_ge(r["selT"], r.at("selT", tt + 1))
                    A(eT[:, tt * P:(tt + 1) * P], bank(4 + tt, 0, P), ACT.Copy).then_inc(r["sel_s"], 1)
                    A(gT[:, tt * P:(tt + 1) * P], bank(4 + tt, P, 2 * P), ACT.Copy).then_inc(r["sel_s"], 1)
                f = full_index(p)

                def gelu(i, h):
                    act.wait_ge(u_free, i * (2 * GRP) + (f * TOK + (h + 1) * GRP + RING))
                    A(ge[:, h, :], hcol[:, h, :], ACT.Gelu).then_inc(gelu_s, 1)

                def put_sums(i, h):
                    act.wait_ge(v_free, i * 2 + (f * 2 * NG + h + 3))
                    act.wait_ge(y_out[h], i * 16 + (f * NG * 16 + 16))
                    A(ystage[:, h, :], PS[0:GRP, (4 + 2 * h) * 512:(6 + 2 * h) * 512], ACT.Copy).then_inc(yc_s, 1)
                    act.wait_ge(yc_s, i * 2 + (f * 2 * NG + h + 3))
                    act.dma_start(ysum[f, bass.ds(i * (2 * GRP) + h * GRP, GRP), :], ystage[:, h, :])\
                        .then_inc(y_out[h], 16)

                for h in range(2):
                    gelu(0, h)
                with act.Fori(0, NG - 1) as i:
                    for h in range(2):
                        put_sums(i, h)
                        gelu(i + 1, h)
                for h in range(2):
                    put_sums(NG - 1, h)
            for tt in range(TT):
                spread(3, "rstat", "rstd", TT + tt + 1)

        @block.vector
        def _(dve):
            V = nc.vector
            ch = Chain(dve, dch_s)
            scr = scratch[:, :, :].rearrange("p t d -> p (t d)")
            dve.sem_inc(u_free, RING)
            dve.wait_ge(rows_t, 1)
            V.tensor_copy(cols[:, 4, 0:16], bank(4, 0, 16)).then_inc(cols_s, 1)
            dve.wait_ge(consts, 16 * 22)
            ch.link(V.tensor_copy(iota_b[:, :], iota[:, :]))

            def stats(src, inc):
                for q in range(2):
                    ch.add(V.bn_stats(bst[:, q, :], src[:, q * 512:(q + 1) * 512]))
                ch.wait()
                V.bn_aggr(mv[:, :], bst[:, :, :]).then_inc(inc, 1)

            def norm(dst, src, std, count, inc=None):
                dve.wait_ge(std, count)
                ch.link(V.reciprocal(sd[:, 1:2], sd[:, 0:1]))
                ins = V.tensor_scalar(dst, src, mv[:, 0:1], sd[:, 1:2], ALU.subtract, ALU.mult)
                if inc is None:
                    ch.link(ins)
                else:
                    ins.then_inc(inc, 1)

            def norm_rows(p, s, base):
                r = R[p]
                for tt in range(TT):
                    stats(X[:, s, tt, :], r["stat"])
                    norm(scratch[:, tt, :], X[:, s, tt, :], r["std"], r.at("std", base + tt + 1), r["xn"])

            def modulation(l):
                dve.wait_ge(mod_p, l + 1)
                badd = cols[:, 2 * l, R_ADA:R_CB].unsqueeze(1).to_broadcast([P, 2, 48])
                ch.link(V.tensor_tensor(mod[:, l, :, :], bank(7, 0, 96).rearrange("p (s n) -> p s n", s=2), badd, ALU.add))
                for q in (8, 32):
                    ch.link(V.tensor_scalar_add(mod[:, l, :, q:q + 8], mod[:, l, :, q:q + 8], 1.0))
                dve.sem_inc(mod_s, 1)

            ln = [0]

            def residual(p, s, base):
                r = R[p]
                ln[0] += 1
                dve.wait_ge(ln_land, 32 * ln[0])
                for tt in range(TT):
                    if base:
                        add = yrows[:, tt, :]
                    else:
                        dve.wait_ge(r["resT"], r.at("resT", tt + 1))
                        add = PS[:, tt * D:(tt + 1) * D]
                    ch.link(V.scalar_tensor_tensor(scratch[:, tt, :], X[:, s, tt, :], ALPHA, add, ALU.mult, ALU.add))
                    stats(scratch[:, tt, :], r["rstat"])
                    norm(scratch[:, tt, :], scratch[:, tt, :], r["rstd"], r.at("rstd", base + tt + 1))
                    ch.link(V.tensor_tensor(scratch[:, tt, :], scratch[:, tt, :], lnrow[:, 0, :], ALU.mult))
                    V.tensor_tensor(X[:, s, tt, :], scratch[:, tt, :], lnrow[:, 1, :], ALU.add).then_inc(r["x_new"], 1)
                    dve.wait_ge(r["x_new"], r.at("x_new", base + tt + 1))

            norm_rows(0, PASSES[0][2], 0)
            dve.wait_ge(rows_t, 2)
            for q, n in enumerate([R_END, 2 * TAPS, R_END, 2 * TAPS]):
                last = V.tensor_copy(cols[:, q, 0:n], bank((1, 3, 5, 6)[q], 0, n))
            last.then_inc(cols_s, 1)
            dve.wait_ge(cols_s, 2)
            for p, (name, l, s, kv) in enumerate(PASSES):
                r = R[p]
                a = 2 * l
                if p and PASSES[p - 1][3]:
                    norm_rows(p, s, 0)
                if not p:
                    modulation(0)
                if p in (0, 2):
                    dve.wait_ge(lrow_s, 48 * (l + 1))
                if p in (0, 3):
                    dve.wait_ge(bias_s, 16 * ROWS * NAT_H * (l + 1))
                    for tt in range(TT):
                        ch.add(V.tensor_tensor(bias[:, tt, :, :], bias[:, tt, :, :],
                                               masks[:, tt, 0:1, :].to_broadcast([P, NAT_H, TOK]), ALU.add))
                    ch.wait()
                units = units_of(s, kv)
                for n, (kind, tile, blk, dst) in enumerate(units):
                    if kind == "N":
                        dve.wait_ge(r["unit"], r.at("unit", n + 1))
                        V.tensor_tensor(nvf[s][:, dst, :], bank(n % 4), brow[:, 0:4 * P], ALU.add)\
                            .then_inc(r["unit_dve"], 1)
                    elif kind == "V":
                        dve.wait_ge(r["unit"], r.at("unit", n + 1))
                        V.tensor_tensor(gvb[s][:, dst, :], bank(n % 4, 0, P), brow[:, 4 * P:5 * P], ALU.add)\
                            .then_inc(r["unit_dve"], 1)
                if kv:
                    continue
                na = sum(u[0] in "TQ" for u in units)
                if s == 0:
                    dve.wait_ge(r["ropemm"], r.at("ropemm", 1))
                    t5 = scr[:, 0:5 * TOK].rearrange("p (q t) -> p q t", q=5)
                    ch.add(V.tensor_tensor(t5, PS[:, 4 * 512:4 * 512 + 5 * TOK].rearrange("p (q t) -> p q t", q=5),
                                           rope[:, 1:2, :].to_broadcast([P, 5, TOK]), ALU.mult))
                    ch.link(V.tensor_tensor(gqk[:, :, :], gqk[:, :, :], rope[:, 0:1, :].to_broadcast([P, 5, TOK]),
                                            ALU.mult))
                    V.tensor_tensor(gqk[:, :, :], gqk[:, :, :], t5, ALU.add).then_inc(r["roped"], 1)
                jobs = attention_jobs()
                w = 2 * TOK if s == 0 else TOK

                def scaled(n):
                    br, h, qt = jobs[n]
                    q = n % 2
                    b_ = SBANK[n % 3]
                    dve.wait_ge(r["S"], r.at("S", n + 1))
                    if s == 0:
                        m_ = bias[:, qt, h, :] if br == 0 else masks[:, qt, 1, :]
                        ch.add(V.scalar_tensor_tensor(Sm[:, q, 0:TOK], bank(b_, 0, TOK), SCALE, m_, ALU.mult, ALU.add))
                        ch.link(V.tensor_scalar(Sm[:, q, TOK:w], bank(b_, TOK, w), SCALE, None, ALU.mult))
                    else:
                        ch.link(V.tensor_scalar(Sm[:, q, 0:w], bank(b_, 0, w), SCALE, None, ALU.mult))
                    ch.link(V.reduce_max(st8[:, q, 0:1], Sm[:, q, 0:w], AX))
                    if br:
                        ch.link(V.tensor_tensor(st8[:, q, 0:1], st8[:, q, 0:1], sink[:, h:h + 1], ALU.max))
                    V.tensor_scalar(st8[:, q, 1:2], st8[:, q, 0:1], -1.0, None, ALU.mult).then_inc(r["sm"], 1)

                def normed(n):
                    br, h, qt = jobs[n]
                    q = n % 2
                    dve.wait_ge(r["exp"], r.at("exp", n + 1))
                    if br:
                        ch.link(V.tensor_tensor(st8[:, q, 2:3], st8[:, q, 2:3], st8[:, q, 3:4], ALU.add))
                    ch.link(V.reciprocal(st8[:, q, 4:5], st8[:, q, 2:3]))
                    V.tensor_scalar(Pn[:, q, 0:w], Pn[:, q, 0:w], st8[:, q, 4:5], None, ALU.mult).then_inc(r["pn"], 1)

                for n in range(len(jobs) + 1):
                    if n < len(jobs):
                        scaled(n)
                    if n:
                        normed(n - 1)
                dve.wait_ge(r["cmean"], r.at("cmean", 1))
                ch.link(V.tensor_tensor(hacc[:, :, :], hacc[:, :, :],
                                        bank(6, 0, TOK).unsqueeze(1).to_broadcast([P, 2, TOK]), ALU.subtract))
                V.tensor_tensor(hsq[:, :, :], hacc[:, :, :], hacc[:, :, :], ALU.mult).then_inc(r["csq"], 1)
                dve.wait_ge(r["xh"], r.at("xh", 1))
                V.tensor_tensor(ul[:, :, :], uT[:, :, :], uh[:, :, :], ALU.subtract).then_inc(r["xl"], 1)
                dve.wait_ge(r["cstd"], r.at("cstd", 1))
                ch.link(V.reciprocal(hstd[:, :], hstd[:, :]))
                V.tensor_tensor(hacc[:, :, :], hacc[:, :, :], hstd[:, :].unsqueeze(1).to_broadcast([P, 2, TOK]),
                                ALU.mult).then_inc(r["cnorm"], 1)
                dve.sem_inc(r["merged"], 2)
                tiles = merge_tiles(p)

                def split_low(i, h, b):
                    dve.wait_ge(r["wh"], r.at("wh", i * 8 + (h * 4 + b + 1)))
                    V.tensor_tensor(low(b), gate_w(tiles[h][0], b), high(b), ALU.subtract).then_inc(r["wl"], 1)

                def merge(i, h, b, ahead):
                    if ahead:
                        split_low(i + ahead[0], ahead[1], ahead[2])
                    mrow = mT[:, bass.ds(i * 2 + h, 1), :].rearrange("p a t -> p (a t)")
                    dve.wait_ge(r["sig"], r.at("sig", i * 8 + (h * 4 + b + 1)))
                    to = mrow if b == 0 else prod[:, b % 2, :]
                    V.tensor_tensor(to, sg[:, b % 2, :], bank(b % 2, TOK, 2 * TOK), ALU.mult)\
                        .then_inc(r["merged"], 1)
                    dve.wait_ge(r["merged"], r.at("merged", i * 8 + (h * 4 + b + 3)))
                    if b:
                        ins = V.tensor_tensor(mrow, mrow, prod[:, b % 2, :], ALU.add)
                        if b == NB - 1:
                            ins.then_inc(r["macc"], 1)
                        else:
                            ch.link(ins)

                split_low(0, 0, 0)
                split_low(0, 0, 1)
                with dve.Fori(0, 3) as i:
                    ch.loop(i, 4)
                    for h, b, ahead in merge_steps():
                        merge(i, h, b, ahead)
                ch.end(3)
                for h, b, ahead in merge_steps():
                    merge(3, h, b, None if ahead[0] else ahead)
                residual(p, s, 0)
                norm_rows(p, s, TT)
                for tt in range(TT):
                    rows_ = PS[:, 4 * 512 + tt * 1024:4 * 512 + (tt + 1) * 1024]
                    dve.wait_ge(r["urow"], r.at("urow", tt + 1))
                    if tt:
                        dve.wait_ge(r["xs_dram"], r.at("xs_dram", 16 * tt))
                    ch.link(V.tensor_copy(xs[:, 0, :], rows_))
                    ch.link(V.tensor_tensor(scratch[:, tt, :], rows_, xs[:, 0, :], ALU.subtract))
                    ch.link(V.tensor_copy(xs[:, 1, :], scratch[:, tt, :]))
                    ch.link(V.tensor_tensor(scratch[:, tt, :], scratch[:, tt, :], xs[:, 1, :], ALU.subtract))
                    V.tensor_copy(xs[:, 2, :], scratch[:, tt, :]).then_inc(r["xsplit"], 1)

                def top16(rows_):
                    for vals, idx, src, spare in rows_:
                        ch.add(V.max(vals[:, 0:8], src))
                    ch.wait()
                    for vals, idx, src, spare in rows_:
                        ch.add(V.max_index(idx[:, 0:8], vals[:, 0:8], src))
                        ch.add(V.match_replace(spare, vals[:, 0:8], src, LOWEST))
                    ch.wait()
                    for vals, idx, src, spare in rows_:
                        ch.add(V.max(vals[:, 8:16], spare))
                    ch.wait()
                    for vals, idx, src, spare in rows_:
                        ch.add(V.max_index(idx[:, 8:16], vals[:, 8:16], spare))
                    ch.wait()

                for t in range(4):
                    dve.wait_ge(r["sc_s"], r.at("sc_s", 2 * t + 2))
                    top16([(v16[:, tt * SEG + g, :], i16[:, tt * SEG + g, :], segs[tt][:, g, :], rest[tt][:, g, :])
                           for tt in range(TT) for g in range(4 * t, 4 * t + 4)])
                dve.sem_inc(r["top"], 1)
                dve.wait_ge(r["xs_dram"], r.at("xs_dram", 16 * TT))
                ch.link(V.tensor_copy(i16f[:, :, :], i16[:, :, :]))
                for tt in range(TT):
                    if tt:
                        dve.wait_ge(r["selT"], r.at("selT", tt))
                    vv = v16[:, tt * SEG:(tt + 1) * SEG, :].rearrange("p (h e) k -> p h e k", e=2)
                    iv = i16f[:, tt * SEG:(tt + 1) * SEG, :].rearrange("p (h e) k -> p h e k", e=2)
                    full = [P, HEADS, TOPK, TOPK]
                    ch.add(V.tensor_tensor(cand[:, :, 0:PAIR_B], vv[:, :, 0, 0:1].to_broadcast([P, HEADS, TOPK]),
                                           vv[:, :, 1, :], ALU.add))
                    mid = [P, HEADS, 7, 8]
                    ch.add(V.tensor_tensor(cand[:, :, PAIR_B:PAIR_C].rearrange("p h (a b) -> p h a b", a=7),
                                           vv[:, :, 0, 1:8].unsqueeze(3).to_broadcast(mid),
                                           vv[:, :, 1, 0:8].unsqueeze(2).to_broadcast(mid), ALU.add))
                    ch.link(V.tensor_tensor(cand[:, :, PAIR_C:PAIRS], vv[:, :, 0, 8:16],
                                            vv[:, :, 1, 0:1].to_broadcast([P, HEADS, 8]), ALU.add))
                    top16([(ts[:, g, :], pos[:, g, :], cand[:, g, :], cand_rest[:, g, :]) for g in range(HEADS)])
                    posu = pos[:, :, :].rearrange("p h k -> p (h k)")
                    ch.add(V.tensor_copy(dec[:, 0, :], posu))
                    ch.link(V.tensor_single_scalar(ab[:, 1, :], posu, 7, ALU.bitwise_and))
                    ch.add(V.tensor_scalar(ab[:, 0, :], dec[:, 0, :], 8.0, -8.0, ALU.max, ALU.add))
                    ch.add(V.tensor_scalar(dec[:, 1, :], dec[:, 0, :], float(PAIR_C), -float(PAIR_C), ALU.max, ALU.add))
                    ch.add(V.tensor_copy(dec[:, 2, :], ab[:, 1, :]))
                    ch.link(V.tensor_scalar(dec[:, 3, :], dec[:, 0, :], 8.0, 8.0, ALU.is_ge, ALU.mult))
                    ch.add(V.tensor_single_scalar(ab[:, 0, :], ab[:, 0, :], 3, ALU.logical_shift_right))
                    ch.add(V.scalar_tensor_tensor(dec[:, 4, :], dec[:, 0, :], float(PAIR_C), dec[:, 2, :],
                                                  ALU.is_lt, ALU.mult))
                    ch.link(V.scalar_tensor_tensor(dec[:, 5, :], dec[:, 0, :], float(PAIR_B), dec[:, 3, :],
                                                   ALU.is_lt, ALU.mult))
                    ch.add(V.tensor_tensor(abf[:, 0, :], ab[:, 0, :], dec[:, 1, :], ALU.add))
                    ch.link(V.tensor_tensor(abf[:, 1, :], dec[:, 4, :], dec[:, 5, :], ALU.add))
                    one = hot[:, :, :, :].rearrange("p h k a -> p (h k) a")
                    one4 = hot[:, :, :, :]
                    for e in range(2):
                        ch.link(V.tensor_tensor(one, abf[:, e, :].unsqueeze(2).to_broadcast([P, P, TOPK]),
                                                iota_b[:, :].unsqueeze(1).to_broadcast([P, P, TOPK]), ALU.is_equal))
                        ch.link(V.tensor_tensor(one4, one4, iv[:, :, e, :].unsqueeze(2).to_broadcast(full), ALU.mult))
                        ch.link(V.reduce_sum(isel[:, e, :], one, AX))
                    ch.link(V.scalar_tensor_tensor(isel[:, 0, :], isel[:, 0, :], float(NKEY), isel[:, 1, :],
                                                   ALU.mult, ALU.add))
                    ch.link(V.tensor_copy(hsum[:, 0, :], ts[:, :, 0:1].rearrange("p h k -> p (h k)")))
                    top = [P, HEADS, TOPK]
                    V.tensor_tensor(ts[:, :, :], ts[:, :, :], hsum[:, 0, :].unsqueeze(2).to_broadcast(top),
                                    ALU.subtract).then_inc(r["tsub"], 1)
                    dve.wait_ge(r["texp"], r.at("texp", tt + 1))
                    ch.link(V.reduce_sum(hsum[:, 1, :], ts[:, :, :], AX))
                    ch.link(V.reciprocal(hsum[:, 1, :], hsum[:, 1, :]))
                    V.tensor_tensor(ts[:, :, :], ts[:, :, :], hsum[:, 1, :].unsqueeze(2).to_broadcast(top),
                                    ALU.mult).then_inc(r["sel"], 1)
                f = full_index(p)
                dve.wait_ge(r["sel_s"], r.at("sel_s", 2 * TT))
                if p == 1:
                    modulation(1)
                with dve.Fori(0, NG) as i:
                    for h in range(2):
                        for k in range(GRP):
                            dve.wait_ge(xb_s, i * (2 * GRP) + (f * TOK + h * GRP + k + 1))
                            dve.wait_ge(u_land[h * GRP + k], i * 16 + (f * NG * 16 + 16))
                            V.tensor_tensor_reduce(out=junk, in0=Ur[:, h * GRP + k, :],
                                                   in1=PS[:, (k % 2) * 1024:(k % 2 + 1) * 1024], scale=1.0, scalar=0.0,
                                                   op0=ALU.mult, op1=ALU.add, accum_out=hcol[:, h, k:k + 1])\
                                .then_inc(u_free, 1)
                            dve.wait_ge(u_free, i * (2 * GRP) + (f * TOK + h * GRP + k + 1 + RING))
                        dve.wait_ge(gelu_s, i * 2 + (f * 2 * NG + h + 1))
                        dve.wait_ge(v_free, i * 2 + (f * 2 * NG + h + 1))
                        V.tensor_tensor(zcol[:, h, :, :].rearrange("p a b -> p (a b)")[:, 0:(GRP - 1) * 33 + 1:33], ge[:, h, :], gT[:, bass.ds(i * (2 * GRP) + h * GRP, GRP)],
                                        ALU.mult).then_inc(w_s, 1)
                dve.wait_ge(yc_s, 2 + 2 * NG * (f + 1))
                dve.sem_inc(r["g2"], 1)
                if p + 1 < len(PASSES):
                    norm_rows(p + 1, PASSES[p + 1][2], 0)
                dve.wait_ge(r["resT"], r.at("resT", TT + 1))
                dve.wait_ge(y_in, 16 * (f + 1))
                for tt in range(TT):
                    ch.link(V.tensor_tensor(yrows[:, tt, :], yrows[:, tt, :], PS[:, 4 * 512:4 * 512 + D], ALU.mult))
                if p + 1 < len(PASSES):
                    dve.wait_ge(R[p + 1]["xnT"], R[p + 1].at("xnT", TT))
                residual(p, s, TT)


INPUTS = ["x", "c", "ctx", "c_ctx", "w_ada", "b_ada", "w_in", "b_in", "conv_w", "conv_b", "conv_ln_g", "conv_ln_b",
          "nat_rpb", "gqa_sink", "w_branch_a", "w_branch_b", "w_branch_c", "w_branch_d", "w_out", "ln1_g", "ln1_b",
          "peer_wq", "peer_k1", "peer_k2", "ln2_g", "ln2_b"]


def shape_constants():
    import numpy as np
    f = np.float32
    t = np.arange(TOK)
    w = 2 * np.pi * ((t[:, None] * t[None, :]) % TOK) / TOK
    both = np.stack([np.cos(w), np.sin(w)])
    dft = both.reshape(2, TT, P, TOK).transpose(2, 1, 0, 3)
    g = np.arange(DH)
    v = 2 * np.pi * ((g[:, None] * g[None, :]) % DH) / DH
    norm = 1.0 / np.sqrt(TOK * DH)
    dftg = np.zeros((P, 2, P))
    for q in range(2):
        sl = slice(q * DH, (q + 1) * DH)
        dftg[sl, 0, sl] = np.cos(v) * norm
        dftg[sl, 1, sl] = -np.sin(v) * norm
    quarter = DH // 4
    freqs = f(10000.0) ** (-np.arange(quarter, dtype=f) / f(quarter))
    rope = np.zeros((P, 2, TOK), f)
    rot = np.zeros((P, P), f)
    for m in range(P):
        d = m % DH
        ang = ((t // GRID_W) if d < DH // 2 else (t % GRID_W)).astype(f) * freqs[d % quarter]
        rope[m, 0] = np.cos(ang)
        rope[m, 1] = np.sin(ang)
        first = (d % (DH // 2)) < quarter
        if first:
            rot[m + quarter, m] = -1.0
        else:
            rot[m - quarter, m] = 1.0
    col = np.arange(GRID_W)
    start = np.clip(col - 8, 0, GRID_W - 16)
    inside = (col[None, :] >= start[:, None]) & (col[None, :] < start[:, None] + 16)
    nat = np.where(np.tile(inside, (ROWS, ROWS)), 0.0, -1e30)
    band = np.where(np.abs(t[:, None] - t[None, :]) <= 128, 0.0, -1e30)
    masks = np.stack([nat, band]).reshape(2, TT, P, TOK).transpose(2, 1, 0, 3)
    iota = np.tile(np.arange(TOPK), (P, 1))
    out = dict(ident_c=np.eye(P), dft_c=dft, dftg_c=dftg, rope_c=rope, rot_c=rot, mask_c=masks, iota_c=iota)
    return {k: np.ascontiguousarray(a).astype(f) for k, a in out.items()}


def kernel(**inputs):
    import numpy as np
    import concourse.bacc as bacc
    from concourse.bass_utils import run_bass_kernel_spmd

    nc = bacc.Bacc("TRN2", target_bir_lowering=False, num_devices=1)
    arrays = {n: np.ascontiguousarray(inputs[n]) for n in INPUTS}
    arrays.update(shape_constants())
    for n in ("peer_u", "peer_v"):
        for l in range(DEPTH):
            arrays[f"{n}{l}"] = np.ascontiguousarray(inputs[n][l])
    args = {}
    for n, a in arrays.items():
        args[n] = nc.dram_tensor("in_" + n, a.shape, mybir.dt.from_np(a.dtype), kind="ExternalInput").ap()
    out = nc.dram_tensor("out_x", (1, TOK, D), F32, kind="ExternalOutput").ap()
    build(nc, out=out, **args)
    r = run_bass_kernel_spmd(nc, [{"in_" + n: a for n, a in arrays.items()}], core_ids=[0])
    return r.results[0]["out_x"]
```
